# Optimizing a Trainium2 kernel written in Bass

```python
import math
import jax, jax.numpy as jnp
from jax import lax
import numpy as np

D_MODEL = 1024
BATCH = 1
SEQ = 512
DEPTH = 2

CHUNK = 64
N_MIXERS = 2
HEAD_DIM_GDN = 128
N_HEADS_GDN = D_MODEL // HEAD_DIM_GDN
GDN_DIM = N_HEADS_GDN * HEAD_DIM_GDN
CONV_K = 4
HEAD_DIM_FOX = 64
N_HEADS_FOX = D_MODEL // HEAD_DIM_FOX
FOX_DIM = N_HEADS_FOX * HEAD_DIM_FOX
Q_BLOCK = 128
N_GROUPS = 4
EXPERTS_PER_GROUP = 8
TOP_K = 2
D_EXPERT = D_MODEL // 4
EPS = 1e-6

kernel_name = 'hybrid_gdn_fox_hmoe_adaln'

def rms_norm(x, gain=None):
    x32 = x.astype(jnp.float32)
    y = x32 * lax.rsqrt(jnp.mean(x32 * x32, axis=-1, keepdims=True) + EPS)
    if gain is not None:
        y = y * gain.astype(jnp.float32)
    return y.astype(x.dtype)

def l2_norm(x):
    x32 = x.astype(jnp.float32)
    return x32 * lax.rsqrt(jnp.sum(x32 * x32, axis=-1, keepdims=True) + EPS)

def causal_depthwise_conv(x, w):
    C = x.shape[-1]
    return lax.conv_general_dilated(
        x, w[:, None, :].astype(x.dtype), window_strides=(1,), padding=[(CONV_K - 1, 0)],
        dimension_numbers=('NWC', 'WIO', 'NWC'), feature_group_count=C)

def gated_delta_rule(q, k, v, log_alpha, beta):
    f32 = jnp.float32
    B, H, L, Dk = q.shape
    Dv = v.shape[-1]
    n = L // CHUNK
    q = (q.astype(f32) * Dk ** -0.5).reshape(B, H, n, CHUNK, Dk)
    k = k.astype(f32).reshape(B, H, n, CHUNK, Dk)
    v = v.astype(f32).reshape(B, H, n, CHUNK, Dv)
    beta = beta.astype(f32).reshape(B, H, n, CHUNK, 1)
    g = jnp.cumsum(log_alpha.astype(f32).reshape(B, H, n, CHUNK), axis=-1)
    diff = g[..., :, None] - g[..., None, :]
    incl = jnp.tril(jnp.ones((CHUNK, CHUNK), dtype=bool))
    strict = jnp.tril(jnp.ones((CHUNK, CHUNK), dtype=bool), -1)
    decay_incl = jnp.exp(jnp.where(incl, diff, -jnp.inf))
    decay_strict = jnp.where(strict, decay_incl, 0.0)
    kb = k * beta
    a_mat = jnp.einsum('bhnik,bhnjk->bhnij', kb, k) * decay_strict + jnp.eye(CHUNK, dtype=f32)
    u = lax.linalg.triangular_solve(a_mat, v * beta, left_side=True, lower=True)
    w = lax.linalg.triangular_solve(a_mat, kb * jnp.exp(g)[..., None], left_side=True, lower=True)
    qk = jnp.einsum('bhnik,bhnjk->bhnij', q, k) * decay_incl
    qg = q * jnp.exp(g)[..., None]
    g_last = g[..., -1]
    kd = k * jnp.exp(g_last[..., None] - g)[..., None]

    def step(S, xs):
        u_c, w_c, qg_c, qk_c, kd_c, gl_c = xs
        v_new = u_c - jnp.einsum('bhck,bhkv->bhcv', w_c, S)
        o_c = jnp.einsum('bhck,bhkv->bhcv', qg_c, S) + jnp.einsum('bhcs,bhsv->bhcv', qk_c, v_new)
        S = S * jnp.exp(gl_c)[..., None, None] + jnp.einsum('bhck,bhcv->bhkv', kd_c, v_new)
        return S, o_c

    xs = (jnp.moveaxis(u, 2, 0), jnp.moveaxis(w, 2, 0), jnp.moveaxis(qg, 2, 0),
          jnp.moveaxis(qk, 2, 0), jnp.moveaxis(kd, 2, 0), jnp.moveaxis(g_last, 2, 0))
    S0 = jnp.zeros((B, H, Dk, Dv), f32)
    _, o = lax.scan(step, S0, xs)
    return jnp.moveaxis(o, 0, 2).reshape(B, H, L, Dv)

def gdn_mixer(h, w_in, conv_w, a_log, dt_bias, o_gain, w_out):
    B, L, _ = h.shape
    proj = h @ w_in
    qkv, gate, a, b = jnp.split(proj, [3 * GDN_DIM, 4 * GDN_DIM, 4 * GDN_DIM + N_HEADS_GDN], axis=-1)
    qkv = jax.nn.silu(causal_depthwise_conv(qkv, conv_w))
    q, k, v = jnp.split(qkv, 3, axis=-1)
    to_heads = lambda t: t.reshape(B, L, N_HEADS_GDN, HEAD_DIM_GDN).transpose(0, 2, 1, 3)
    q = l2_norm(to_heads(q))
    k = l2_norm(to_heads(k))
    v = to_heads(v)
    beta = jax.nn.sigmoid(b.astype(jnp.float32)).transpose(0, 2, 1)
    log_alpha = (-jnp.exp(a_log.astype(jnp.float32))
                 * jax.nn.softplus(a.astype(jnp.float32) + dt_bias.astype(jnp.float32))).transpose(0, 2, 1)
    o = gated_delta_rule(q, k, v, log_alpha, beta).astype(h.dtype)
    o = o.transpose(0, 2, 1, 3)
    o = rms_norm(o, o_gain) * jax.nn.silu(gate.reshape(B, L, N_HEADS_GDN, HEAD_DIM_GDN))
    return o.reshape(B, L, GDN_DIM) @ w_out

def fox_mixer(h, w_in, b_f, q_gain, k_gain, w_out):
    B, L, _ = h.shape
    proj = h @ w_in
    q, k, v, g_out, f_logit = jnp.split(proj, [FOX_DIM, 2 * FOX_DIM, 3 * FOX_DIM, 4 * FOX_DIM], axis=-1)
    to_heads = lambda t: t.reshape(B, L, N_HEADS_FOX, HEAD_DIM_FOX)
    q = rms_norm(to_heads(q), q_gain).transpose(0, 2, 1, 3)
    k = rms_norm(to_heads(k), k_gain).transpose(0, 2, 1, 3)
    v = to_heads(v).transpose(0, 2, 1, 3)
    log_f = jax.nn.log_sigmoid(f_logit.astype(jnp.float32) + b_f.astype(jnp.float32))
    cum = jnp.cumsum(log_f, axis=1).transpose(0, 2, 1)
    scale = HEAD_DIM_FOX ** -0.5
    outs = []
    for blk in range(L // Q_BLOCK):
        q0 = blk * Q_BLOCK
        q1 = q0 + Q_BLOCK
        s = jnp.einsum('bhqd,bhkd->bhqk', q[:, :, q0:q1], k[:, :, :q1]).astype(jnp.float32) * scale
        s = s + cum[:, :, q0:q1, None] - cum[:, :, None, :q1]
        mask = jnp.arange(q1)[None, :] <= jnp.arange(q0, q1)[:, None]
        p = jax.nn.softmax(jnp.where(mask, s, -jnp.inf), axis=-1).astype(v.dtype)
        outs.append(jnp.einsum('bhqk,bhkd->bhqd', p, v[:, :, :q1]))
    o = jnp.concatenate(outs, axis=2).transpose(0, 2, 1, 3).reshape(B, L, FOX_DIM)
    o = o * jax.nn.sigmoid(g_out)
    return o @ w_out

def hier_moe(h, w_group, b_group, w_router, b_router, w_gate_up, w_down):
    B, L, D = h.shape
    t = h.reshape(-1, D)
    T = t.shape[0]
    f32 = jnp.float32
    g_prob = jax.nn.softmax((t @ w_group + b_group).astype(f32), axis=-1)
    g_p, g_idx = lax.top_k(g_prob, 1)
    e_logits = (t @ w_router + b_router).astype(f32).reshape(T, N_GROUPS, EXPERTS_PER_GROUP)
    e_sel = jnp.take_along_axis(e_logits, g_idx[:, :, None], axis=1)[:, 0]
    e_top, e_idx = lax.top_k(e_sel, TOP_K)
    e_w = jax.nn.softmax(e_top, axis=-1) * g_p
    e_comb = jnp.einsum('tk,tke->te', e_w, jax.nn.one_hot(e_idx, EXPERTS_PER_GROUP, dtype=f32))
    combine = (jax.nn.one_hot(g_idx[:, 0], N_GROUPS, dtype=f32)[:, :, None]
               * e_comb[:, None, :]).astype(h.dtype)
    y = jnp.zeros_like(t)
    for gi in range(N_GROUPS):
        hu = jnp.einsum('td,edf->tef', t, w_gate_up[gi])
        gate, up = jnp.split(hu, 2, axis=-1)
        act = jax.nn.silu(gate) * up * combine[:, gi, :, None]
        y = y + jnp.einsum('tef,efd->td', act, w_down[gi])
    return y.reshape(B, L, D)

def setup_inputs(seed: int = 0) -> dict:
    key = jax.random.key(seed)
    ks = jax.random.split(key, 24)
    nrm = lambda k, shape, s: jax.random.normal(k, shape, jnp.float32) * s
    n_a = (DEPTH + 1) // N_MIXERS
    n_b = DEPTH // N_MIXERS
    gdn_in = 4 * GDN_DIM + 2 * N_HEADS_GDN
    fox_in = 4 * FOX_DIM + N_HEADS_FOX
    dt = jnp.exp(jax.random.uniform(ks[7], (n_a, N_HEADS_GDN), jnp.float32,
                                    minval=math.log(1e-3), maxval=math.log(1e-1)))
    return {
        'x': nrm(ks[0], (BATCH, SEQ, D_MODEL), 1.0),
        'c': nrm(ks[1], (BATCH, D_MODEL), 1.0),
        'ada_w': nrm(ks[2], (DEPTH, D_MODEL, 6 * D_MODEL), 0.5 * D_MODEL ** -0.5),
        'ada_b': nrm(ks[3], (DEPTH, 6 * D_MODEL), 0.02),
        'gdn_w_in': nrm(ks[4], (n_a, D_MODEL, gdn_in), D_MODEL ** -0.5),
        'gdn_conv': nrm(ks[5], (n_a, CONV_K, 3 * GDN_DIM), CONV_K ** -0.5),
        'gdn_a_log': jnp.log(jax.random.uniform(ks[6], (n_a, N_HEADS_GDN), jnp.float32, minval=1.0, maxval=16.0)),
        'gdn_dt_bias': dt + jnp.log(-jnp.expm1(-dt)),
        'gdn_norm': 1.0 + nrm(ks[8], (n_a, HEAD_DIM_GDN), 0.02),
        'gdn_w_out': nrm(ks[9], (n_a, GDN_DIM, D_MODEL), GDN_DIM ** -0.5),
        'fox_w_in': nrm(ks[10], (n_b, D_MODEL, fox_in), D_MODEL ** -0.5),
        'fox_b_f': 3.0 + nrm(ks[11], (n_b, N_HEADS_FOX), 0.5),
        'fox_q_norm': 1.0 + nrm(ks[12], (n_b, HEAD_DIM_FOX), 0.02),
        'fox_k_norm': 1.0 + nrm(ks[13], (n_b, HEAD_DIM_FOX), 0.02),
        'fox_w_out': nrm(ks[14], (n_b, FOX_DIM, D_MODEL), FOX_DIM ** -0.5),
        'moe_w_group': nrm(ks[15], (DEPTH, D_MODEL, N_GROUPS), D_MODEL ** -0.5),
        'moe_b_group': nrm(ks[16], (DEPTH, N_GROUPS), 0.01),
        'moe_w_router': nrm(ks[17], (DEPTH, D_MODEL, N_GROUPS * EXPERTS_PER_GROUP), D_MODEL ** -0.5),
        'moe_b_router': nrm(ks[18], (DEPTH, N_GROUPS * EXPERTS_PER_GROUP), 0.01),
        'moe_w_gate_up': nrm(ks[19], (DEPTH, N_GROUPS, EXPERTS_PER_GROUP, D_MODEL, 2 * D_EXPERT), D_MODEL ** -0.5),
        'moe_w_down': nrm(ks[20], (DEPTH, N_GROUPS, EXPERTS_PER_GROUP, D_EXPERT, D_MODEL), D_EXPERT ** -0.5),
        'final_norm': 1.0 + nrm(ks[21], (D_MODEL,), 0.02),
    }

def reference(x, c, ada_w, ada_b, gdn_w_in, gdn_conv, gdn_a_log, gdn_dt_bias, gdn_norm, gdn_w_out,
              fox_w_in, fox_b_f, fox_q_norm, fox_k_norm, fox_w_out,
              moe_w_group, moe_b_group, moe_w_router, moe_b_router, moe_w_gate_up, moe_w_down,
              final_norm):
    c_act = jax.nn.silu(c)
    for i in range(DEPTH):
        ada = (c_act @ ada_w[i] + ada_b[i])[:, None, :]
        sh1, sc1, g1, sh2, sc2, g2 = jnp.split(ada, 6, axis=-1)
        h = rms_norm(x) * (1.0 + sc1) + sh1
        j = i // N_MIXERS
        if i % N_MIXERS == 0:
            y = gdn_mixer(h, gdn_w_in[j], gdn_conv[j], gdn_a_log[j], gdn_dt_bias[j], gdn_norm[j], gdn_w_out[j])
        else:
            y = fox_mixer(h, fox_w_in[j], fox_b_f[j], fox_q_norm[j], fox_k_norm[j], fox_w_out[j])
        x = x + g1 * y
        h = rms_norm(x) * (1.0 + sc2) + sh2
        x = x + g2 * hier_moe(h, moe_w_group[i], moe_b_group[i], moe_w_router[i], moe_b_router[i],
                              moe_w_gate_up[i], moe_w_down[i])
    return rms_norm(x, final_norm)


_drawn_inputs = setup_inputs


def setup_inputs(seed=0):
    import zlib

    import numpy as np

    out = dict(_drawn_inputs(seed))
    spreads = {}
    factors = {'gdn_norm': 6.449,
     'fox_b_f': 21.624,
     'fox_q_norm': 33.433,
     'fox_k_norm': 30.823,
     'moe_b_group': 30.096,
     'moe_b_router': 26.563,
     'final_norm': 7.515}
    for name, (base, spread) in spreads.items():
        noise = np.random.default_rng([zlib.crc32(name.encode()), seed]).standard_normal(out[name].shape)
        drawn = base * np.exp(spread * noise) if base else spread * noise
        out[name] = __import__('jax').numpy.asarray(drawn.astype(out[name].dtype))
    for name, factor in factors.items():
        out[name] = (out[name] * factor).astype(out[name].dtype)
    return out
```

```python
from contextlib import ExitStack

import numpy as np

import concourse.bass as bass
from concourse import mybir

F32 = mybir.dt.float32
I32 = mybir.dt.int32
ALU = mybir.AluOpType
ACT = mybir.ActivationFunctionType
AX_X = mybir.AxisListType.X

P = 128
T, D = 512, 1024
NT, KD = T // P, D // P
H = 8
NG, EPG = 4, 8
NE = NG * EPG
DE = 256
CONV = 4
LEVELS = 7
EPS = 1e-6
ADA_W = 256
ADA_FIRST = 8
ADA_PER_HEAD = 5
NEG = -1e30
MORE = 7
NO_ROW = 8192
GDN, FOX = 0, 1


def ds(i, n):
    return bass.ds(i, n)


class Link:

    def __init__(self, eng, sem, passed=None):
        self.eng, self.sem, self.base, self.k, self.passed = eng, sem, 0, 0, passed

    def __call__(self, ins):
        self.k += 1
        ins.then_inc(self.sem, 1)
        self.eng.wait_ge(self.sem, self.base + self.k)
        if self.passed is not None and not isinstance(self.base, int):
            self.eng.sem_inc(self.passed, 1)

    def enter(self, i, per):
        self.start, self.per = self.base + self.k, per
        self.base, self.k = i * per + self.start, 0

    def leave(self, n):
        assert self.k == self.per, f"links per iteration: {self.k}"
        self.base, self.k = self.start + n * self.per, 0


def after(eng, sem, n):
    if not isinstance(n, int) or n > 0:
        eng.wait_ge(sem, n)


def build(nc, x, c, ada_w, ada_b, gdn_w_in, gdn_conv, gdn_a_log, gdn_dt_bias, gdn_norm, gdn_w_out,
          fox_w_in, fox_b_f, fox_q_norm, fox_k_norm, fox_w_out, moe_w_group, moe_b_group,
          moe_w_router, moe_b_router, moe_w_gate_up, moe_w_down, final_norm, out):
    ctx = ExitStack()
    with ctx:
        def sb(name, shape, dt=F32):
            return ctx.enter_context(nc.sbuf_tensor(name, shape, dt))

        def sem(name):
            return ctx.enter_context(nc.semaphore(name))

        def sems(name, n):
            return [sem(f"{name}{i}") for i in range(n)]

        ada_rows = nc.dram_tensor("ada_rows", (2, 6 * D), F32, kind="Internal").ap()
        h_rows = [nc.dram_tensor(f"h_rows{i}", (T, D), F32, kind="Internal").ap() for i in range(2)]
        y_rows = [nc.dram_tensor(f"y_rows{i}", (2 * T, D), F32, kind="Internal").ap() for i in range(2)]

        X = sb("X", [P, NT, D])
        hT = sb("hT", [P, KD, T])
        Wr = sb("Wr", [P, 4, KD, 512])
        Dr = sb("Dr", [P, 2, 2048])
        shiftB = sb("shiftB", [P, D])
        scaleB = sb("scaleB", [P, D])
        gateB = sb("gateB", [P, D])
        ident = sb("ident", [P, P])
        ones = sb("ones", [P, P])
        upto = sb("upto", [P, P])
        before = sb("before", [P, P])
        halves = sb("halves", [P, P])
        negmask = sb("negmask", [P, LEVELS, P])
        rows_in = sb("rows_in", [P, P])
        cols = sb("cols", [P, P])
        cact = sb("cact", [P, KD])
        nega = sb("nega", [P, H])
        dtb = sb("dtb", [P, H])
        bfb = sb("bfb", [P, 2 * H])
        routB = sb("routB", [P, 2, NG + NE])
        routW = sb("routW", [P, 2, KD, NG + NE])
        abW = sb("abW", [P, KD, 2 * H])
        fW = sb("fW", [P, KD, 2 * H])
        taps = sb("taps", [P, 3 * CONV])
        iota_i = sb("iota_i", [P, NE], I32)
        iota_e = sb("iota_e", [P, NE])
        iota_r = sb("iota_r", [P, P])
        dest1 = sb("dest1", [P, 2, NT])
        bias_row = sb("bias_row", [P, 2, ADA_W])
        ada_acc = sb("ada_acc", [P, 2, ADA_W])
        ada_row = sb("ada_row", [1, 2, ADA_W])
        ss = sb("ss", [P, NT])
        rstd = sb("rstd", [P, NT])
        eps_c = sb("eps_c", [P, 4])
        AR = 33 * 512
        arena = sb("arena", [P, AR])

        class Carve:

            def __init__(self, at=0):
                self.at = at

            def __call__(self, *shape, dt=None):
                n = int(np.prod(shape))
                v = arena[:, self.at:self.at + n]
                self.at += n
                assert self.at <= AR, self.at
                if dt is not None:
                    v = v.bitcast(dt)
                if len(shape) == 2:
                    v = v.rearrange("p (a b) -> p a b", a=shape[0])
                if len(shape) == 3:
                    v = v.rearrange("p (a b c) -> p a b c", a=shape[0], b=shape[1])
                return v

        cv = Carve()
        OT = cv(KD, T)
        after_ot = cv.at
        cv = Carve(after_ot)
        hrow = [cv(D) for _ in range(2)]
        sq_junk = cv(D)
        cv = Carve(after_ot)
        cin = [cv(T + CONV - 1) for _ in range(2)]
        cv.at += 2
        qkv = [cv(T) for _ in range(3)]
        gate_s = cv(T)
        sqk, sqq = cv(T), cv(T)
        egB, dT = cv(T), cv(T)
        khat, qhat, kb, qg = cv(T), cv(T), cv(T), cv(T)
        vb, kwn, kdec_k = cv(T), cv(T), cv(T)
        XiT = cv(T)
        aT, qkT, Xi = sqk, sqq, egB
        nt = [XiT] + [cv(T) for _ in range(LEVELS - 2)] + [khat]
        vnew = cv(2, P)
        S = cv(P)
        la, gc, beta, nbeg, kdecay, egl, t_ab, t_ab2 = (cv(H * NT) for _ in range(8))
        lah = cv(2, NT)
        Pp, nWT, osq, rB, t1 = kb, qhat, egB, dT, khat
        cv = Carve(after_ot)
        qkr = [cv(T) for _ in range(2)]
        sqr = [cv(T) for _ in range(2)]
        vraw, eg, vS, sgate, on = cv(NT, P), cv(NT, P), cv(NT, P), cv(NT, P), cv(NT, P)
        qh, kh = cv(T), cv(T)
        cbS = cv(2, T)
        offs = [0, 128, 384, 768]
        cbT = [cv(1280) for _ in range(2)]
        sS = [cv(T) for _ in range(2)]
        pS = [cv(T) for _ in range(2)]
        pT = [cv(T) for _ in range(2)]
        cumn = cv(NT * 2 * H)
        lf, tf1, tf2 = pS[0][:, 0:NT * 2 * H], sS[0][:, 0:NT * 2 * H], sS[1][:, 0:NT * 2 * H]
        nch = cv(2, NT)
        mx, nmx, rsum = cv(8), cv(8), cv(8)
        rinv = cv(8)
        cv = Carve()
        xg = [cv(D) for _ in range(4)]
        xgT = [cv(KD, P) for _ in range(2)]
        sg = [cv(DE) for _ in range(2)]
        ac = [cv(DE) for _ in range(2)]
        acT = [cv(2, P) for _ in range(2)]
        yo = [cv(D) for _ in range(2)]
        assert cv.at <= 12288
        place1 = cv(2 * NT, P)
        lt = cv(NE, NE)
        cv.at = 12288
        lg = cv(NT, NG + NE)
        gm, gz, gp, m1, m2, e21, w1, w2 = (cv(NT) for _ in range(8))
        geq, gidx = cv(NT, NG), cv(NT, NG)
        el, oh1, oh2, both, rank, tmp32 = (cv(NT, NE) for _ in range(6))
        ohd = [cv(NT, NE) for _ in range(2)]
        mi = cv(NT)
        posf = cv(2, NT)
        posb = cv(2, NT)
        slot_f = cv(NT * NE)
        slot_t = cv(NT * NE)
        slot_i = cv(NT * NE, dt=I32)
        slot_g = cv(NT * NE, dt=I32)
        over_n, before_n = cv(NE), cv(NE)
        item_d, item_s, item_v = cv(MORE, NE), cv(MORE, NE), cv(MORE, NE)
        item_f = cv(3, MORE)
        item_i = cv(2 * MORE, dt=I32)
        nextra = cv(1, dt=I32)
        sidx = cv(2, 1, dt=I32)
        gidx_i = cv(4, 1, dt=I32)
        place2 = cv(2 * NT, P)
        Y = arena[:, 0:8 * D].rearrange("p (k n d) -> p k n d", k=2, n=NT)

        PS = [ctx.enter_context(nc.psum_tensor(f"PS{i}", [P, 512], F32)) for i in range(8)]

        consts = sem("consts")
        small_in, small2_in = sem("small_in"), sem("small2_in")
        x_in = sem("x_in")
        cols_ps, cols_ok = sem("cols_ps"), sem("cols_ok")
        act_setup = sem("act_setup")
        dve_link, act_link, pool_link = sem("dve_link"), sem("act_link"), sem("pool_link")
        pool_passed, dve_passed = sem("pool_passed"), sem("dve_passed")
        ada_in = sems("ada_in", 2)
        ada_sum = sem("ada_sum")
        ada_sum2 = sem("ada_sum2")
        ada_ps, ada_rowok = sem("ada_ps"), sem("ada_rowok")
        ada_out = sems("ada_out", 2)
        bc_in = sem("bc_in")
        gate_in = sem("gate_in")
        gdn_w, fox_w = sems("gdn_w", 2), sems("fox_w", 2)
        moe_w = sems("moe_w", 4)
        moe_d = sems("moe_d", 2)
        n_rs, n_h, n_tr, n_ta, n_tb = sem("n_rs"), sem("n_h"), sem("n_tr"), sem("n_ta"), sem("n_tb")
        proj_ps = sem("proj_ps")
        ev_pj = sem("ev_pj")
        conv_ok = sem("conv_ok")
        sq_ok = sem("sq_ok")
        decay_ps, decay_act, decay_dve = sem("decay_ps"), sem("decay_act"), sem("decay_dve")
        row_ok, gb_ps, ss_ps = sem("row_ok"), sem("gb_ps"), sem("ss_ps")
        rr_ok = sem("rr_ok")
        diff_ok, msk_ok, dT_ok, egb_ok = sem("diff_ok"), sem("msk_ok"), sem("dT_ok"), sem("egb_ok")
        hat_ok, kb_ok, qg_ok = sem("hat_ok"), sem("kb_ok"), sem("qg_ok")
        v_ps, k_ps, kk_ps, qk_ps = sem("v_ps"), sem("k_ps"), sem("kk_ps"), sem("qk_ps")
        vb_ok, kd_ok, at_ok, qkt_ok, xt_ok = sem("vb_ok"), sem("kd_ok"), sem("at_ok"), sem("qkt_ok"), sem("xt_ok")
        nt_ok, x1_ps, x1_ok, p_ps, p_ok, lv_ps, lv_ok = (sem(n) for n in ("nt_ok", "x1_ps", "x1_ok", "p_ps", "p_ok", "lv_ps", "lv_ok"))
        wt_ps, wt_ok, vn_ps, vn_ok, s_ps, s_ok = (sem(n) for n in ("wt_ps", "wt_ok", "vn_ps", "vn_ok", "s_ps", "s_ok"))
        o_ps, osq_ok, sso_ps, ro_ok, ot_ok = (sem(n) for n in ("o_ps", "osq_ok", "sso_ps", "ro_ok", "ot_ok"))
        wo_ps, wo_ok = sem("wo_ps"), sem("wo_ok")
        forget_ps, forget_act, forget_dve = sem("forget_ps"), sem("forget_act"), sem("forget_dve")
        fpj_ps, fev = sem("fpj_ps"), sem("fev")
        fs_ps, fr_ok, qkh_ok = sem("fs_ps"), sem("fr_ok"), sem("qkh_ok")
        nch_ok, vs_ok, sgt_ok = sem("nch_ok"), sem("vs_ok"), sem("sgt_ok")
        cb_ps, cb_ok, cbt_ok = sem("cb_ps"), sem("cb_ok"), sem("cbt_ok")
        sc_ps, sc_ok, pr_ok, pt_ps, pt_ok, pv_ps = (sem(n) for n in ("sc_ps", "sc_ok", "pr_ok", "pt_ps", "pt_ok", "pv_ps"))
        on_ok, ont_ps, ont_ok = sem("on_ok"), sem("ont_ps"), sem("ont_ok")
        r_ps, r_m, r_e, r_w, r_both, r_rank, r_pos, idx_ok = (sem(n) for n in ("r_ps", "r_m", "r_e", "r_w", "r_both", "r_rank", "r_pos", "idx_ok"))
        hr_out, y_in = sems("hr_out", 2), sems("y_in", NT)
        slots_ps = sem("slots_ps")
        fin_w, fin_ok, fin_out = sem("fin_w"), sem("fin_ok"), sem("fin_out")
        STAGES = ("idx", "xt_ps", "xt", "gu_ps", "sg", "ac", "at_ps", "at", "dn_ps", "y")
        stage_n = lambda name, j: j * len(STAGES) + (STAGES.index(name) + 1)
        M = {n: sem(f"moe_{n}") for n in ("xt_ps", "xt_a", "xt_b", "gu_ps", "sg", "ac", "at_ps", "at", "dn_ps", "ya", "yb", "cp")}
        M["xg"] = sems("moe_xg", 4)
        M["y"] = sems("moe_y", 2)
        M["done"] = sem("moe_done")
        MX = [{n: sem(f"more{i}_{n}") for n in ("w", "moved", "next", "stage")} for i in range(2)]

        block = ctx.enter_context(nc.Block())
        t4 = lambda ap: ap.rearrange("p (n j) -> p n j", n=NT)
        over = lambda ap: ap.unsqueeze(2).to_broadcast([P, NT, P])

        ada_v = ada_w.rearrange("l (k p) n -> l p k n", p=P)

        @block.sync
        def _(sp):
            def load(dst, src, s):
                sp.dma_start(dst, src).then_inc(s, 16)

            def ada_load(a, layer, col, free_sem, free_n):
                slot = a % 2
                after(sp, free_sem, free_n)
                load(Dr[:, slot, :].rearrange("p (k n) -> p k n", k=KD), ada_v[layer, :, :, ds(col, ADA_W)], ada_in[slot])
                load(bias_row[0:1, slot, :], ada_b[layer:layer + 1, ds(col, ADA_W)], ada_in[slot])

            def section_loads(w, h, slot, s):
                for m in range(4):
                    load(Wr[:, slot, :, m * P:m * P + P],
                         w[0, :, m * D:(m + 1) * D].rearrange("(k p) n -> p k n", p=P)[:, :, ds(h * P, P)], s)

            sp.wait_ge(consts, 1)
            load(rows_in[0:CONV * 24, :], gdn_conv.rearrange("a j (m p) -> (a j m) p", p=P), small_in)
            load(rows_in[96:104, :], c.rearrange("a (k p) -> (a k) p", p=P), small_in)
            load(rows_in[104:105, :], gdn_norm, small_in)
            for half in range(2):
                load(rows_in[105:106, 64 * half:64 * half + 64], fox_q_norm, small_in)
                load(rows_in[106:107, 64 * half:64 * half + 64], fox_k_norm, small_in)
            load(nega[:], gdn_a_log[0].partition_broadcast(P), small_in)
            load(dtb[:], gdn_dt_bias[0].partition_broadcast(P), small_in)
            load(bfb[:], fox_b_f[0].partition_broadcast(P), small_in)
            for a in range(2):
                ada_load(a, 0, a * ADA_W, ada_sum, 0)
            load(X[:], x.rearrange("a (n p) d -> p (a n) d", p=P), x_in)
            for a in range(2, ADA_FIRST):
                ada_load(a, 0, a * ADA_W, ada_sum, a - 1)
            section_loads(gdn_w_in, 0, 0, gdn_w[0])
            load(abW[:], gdn_w_in[0, :, 4 * D:].rearrange("(k p) n -> p k n", p=P), small2_in)
            load(fW[:], fox_w_in[0, :, 4 * D:].rearrange("(k p) n -> p k n", p=P), small2_in)
            for i in range(2):
                load(routB[:, i, 0:NG], moe_b_group[i].partition_broadcast(P), small2_in)
                load(routB[:, i, NG:], moe_b_router[i].partition_broadcast(P), small2_in)
                load(routW[:, i, :, 0:NG], moe_w_group[i].rearrange("(k p) n -> p k n", p=P), small2_in)
                load(routW[:, i, :, NG:], moe_w_router[i].rearrange("(k p) n -> p k n", p=P), small2_in)
            for s in range(2):
                sp.wait_ge(ada_out[s], 16 * (ADA_FIRST // 2))
            load(shiftB[:], ada_rows[0, 0:D].partition_broadcast(P), bc_in)
            load(scaleB[:], ada_rows[0, D:2 * D].partition_broadcast(P), bc_in)
            section_loads(gdn_w_in, 1, 1, gdn_w[1])

            def expert_load(i, e, slot):
                load(Wr[:, slot], moe_w_gate_up[i].rearrange("g e (k p) n -> (g e) p k n", p=P)[ds(e, 1)]
                     .rearrange("a p k n -> p (a k) n"), moe_w[slot])

            def down_load(i, e, slot):
                load(Dr[:, slot, :].rearrange("p (k n) -> p k n", k=2),
                     moe_w_down[i].rearrange("g e (k p) n -> (g e) p k n", p=P)[ds(e, 1)]
                     .rearrange("a p k n -> p (a k) n"), moe_d[slot])

            def ada_of_head(d, par):
                for q in range(ADA_PER_HEAD):
                    a = par + q
                    layer, col = (0, (d * 2 + 8 + q) * ADA_W) if q < 2 else (1, (d * 3 + (q - 2)) * ADA_W)
                    n = d * ADA_PER_HEAD + q - 1
                    if isinstance(n, int) and n <= 0:
                        ada_load(a, layer, col, ada_sum, ADA_FIRST + n)
                    else:
                        ada_load(a, layer, col, ada_sum2, n)

            def head_load(h, slot):
                sp.wait_ge(proj_ps, (h - 1) * 4)
                section_loads(gdn_w_in, h, slot, gdn_w[slot])

            for e in range(2):
                expert_load(0, e, e + 2)
            ada_of_head(0, 0)
            head_load(2, 0)
            with sp.Fori(0, 2) as j:
                for u in range(2):
                    ada_of_head(j * 2 + (1 + u), (1 + u) % 2)
                    head_load(j * 2 + (3 + u), (1 + u) % 2)
            ada_of_head(5, 1)
            head_load(7, 1)

            def out_load(w, nh, slot, s):
                load(Wr[:, slot], w[0].rearrange("(k p) n -> p k n", p=P)[:, :, nh * 512:nh * 512 + 512], s)

            ada_of_head(6, 0)
            sp.wait_ge(proj_ps, 4 * 7)
            out_load(gdn_w_out, 0, 0, gdn_w[0])
            ada_of_head(7, 1)
            sp.wait_ge(proj_ps, 4 * 8)
            out_load(gdn_w_out, 1, 1, gdn_w[1])

            def sublayer_rows(layer):
                for s in range(2):
                    if layer == 0:
                        sp.wait_ge(ada_out[s], 16 * 3 * H)
                if layer == 1:
                    sp.wait_ge(wo_ok, 2 * NT + 1)
                load(gateB[:], ada_rows[layer, 2 * D:3 * D].partition_broadcast(P), gate_in)
                sp.wait_ge(n_h, 4 * 2 * layer + 4)
                load(shiftB[:], ada_rows[layer, 3 * D:4 * D].partition_broadcast(P), bc_in)
                load(scaleB[:], ada_rows[layer, 4 * D:5 * D].partition_broadcast(P), bc_in)

            def experts(i):
                m = M
                B = i * NE
                sp.wait_ge(wo_ps, (i + 1) * 2 * NT)
                if i == 0:
                    sp.wait_ge(ada_sum2, ADA_PER_HEAD * H)
                for e in range(2):
                    down_load(i, e, e)
                for e in range(2, 4):
                    expert_load(i, e, e - 2)
                for n in range(NT):
                    sp.wait_ge(n_h, 4 * (2 * i + 1) + n + 1)
                    load(h_rows[i][n * P:n * P + P, :], hrow[n % 2], hr_out[n % 2])
                sp.wait_ge(wo_ok, i * (2 * NT + 1) + 2 * NT)
                load(gateB[:], ada_rows[i, 5 * D:6 * D].partition_broadcast(P), gate_in)
                with sp.Fori(0, NE // 4 - 1) as j:
                    for u in range(4):
                        sp.wait_ge(m["gu_ps"], j * 4 + u + 1 + B)
                        expert_load(i, j * 4 + (u + 4), (u + 2) % 4)
                        sp.wait_ge(m["dn_ps"], j * 4 + u + 1 + B)
                        down_load(i, j * 4 + (u + 2), u % 2)
                for e in range(NE - 2, NE):
                    sp.wait_ge(m["dn_ps"], e + (B - 1))
                    down_load(i, e, e % 2)
                sp.wait_ge(m["dn_ps"], B + NE - 1)
                xm = MX[i]
                sp.wait_ge(idx_ok, 2 * i + 2)
                n_x = sp.value_load(nextra[0:1, 0:1], min_val=0, max_val=MORE)
                with sp.If(n_x > 0):
                    with sp.Fori(0, n_x) as j:
                        e = sp.value_load(item_i[0:1, ds(j, 1)], min_val=0, max_val=NE - 1)
                        sp.wait_ge(xm["next"], j + 1)
                        load(Wr[:, 2], moe_w_gate_up[i].rearrange("g e (k p) n -> (g e) p k n", p=P)[ds(e, 1)]
                             .rearrange("a p k n -> p (a k) n"), xm["w"])
                        load(Dr[:, 0, :].rearrange("p (k n) -> p k n", k=2),
                             moe_w_down[i].rearrange("g e (k p) n -> (g e) p k n", p=P)[ds(e, 1)]
                             .rearrange("a p k n -> p (a k) n"), xm["w"])
                with sp.Else():
                    sp.nop()
                sp.nop()

            def combine_load(i):
                sp.wait_ge(M["done"], i + 1)
                for n in range(NT):
                    for k in range(2):
                        load(Y[:, k, n, :], y_rows[i][k * T + n * P:k * T + n * P + P, :], y_in[n])

            sublayer_rows(0)
            experts(0)
            def pair_load(p, slot, n):
                after(sp, fpj_ps, n * 4)
                section_loads(fox_w_in, p, slot, fox_w[slot])

            sp.wait_ge(n_h, 8)
            load(shiftB[:], ada_rows[1, 0:D].partition_broadcast(P), bc_in)
            load(scaleB[:], ada_rows[1, D:2 * D].partition_broadcast(P), bc_in)
            pair_load(0, 0, 0)
            combine_load(0)
            pair_load(1, 1, 0)
            for e in range(2):
                expert_load(1, e, e + 2)
            with sp.Fori(0, 3) as j:
                for u in range(2):
                    pair_load(j * 2 + (2 + u), u, j * 2 + (1 + u))
            for u in range(2):
                sp.wait_ge(fpj_ps, 4 * (7 + u))
                out_load(fox_w_out, u, u, fox_w[u])
            sublayer_rows(1)
            experts(1)
            sp.wait_ge(n_h, 16)
            load(shiftB[:], final_norm.partition_broadcast(P), fin_w)
            combine_load(1)
            for n in range(NT):
                sp.wait_ge(fin_ok, n + 1)
                load(out[0, n * P:n * P + P, :], X[:, n, :], fin_out)
            sp.wait_ge(fin_out, 16 * NT)

        @block.tensor
        def _(pe):
            mm = nc.tensor.matmul
            tr = nc.tensor.transpose

            def tile(ap, n):
                return ap[:, n * P:n * P + P]

            def norm_transposes(phase):
                for n in range(NT):
                    pe.wait_ge(n_h, 4 * phase + n + 1)
                    if n >= 2:
                        pe.wait_ge(n_ta, 4 * phase + n - 1)
                        pe.wait_ge(n_tb, 4 * phase + n - 1)
                    for k in range(KD):
                        last = tr(PS[2 * (n % 2) + k // 4][:, (k % 4) * P:(k % 4) * P + P],
                                  hrow[n % 2][:, k * P:k * P + P], ident[:])
                    last.then_inc(n_tr, 1)

            def hT_ready(phase):
                pe.wait_ge(n_ta, 4 * phase + 4)
                pe.wait_ge(n_tb, 4 * phase + 4)

            def narrow(w, width, done):
                for n in range(NT):
                    for k in range(KD):
                        last = mm(PS[4][:, n * width:(n + 1) * width], tile(hT[:, k, :], n), w[:, k, :],
                                  start=(k == 0), stop=(k == KD - 1))
                last.then_inc(done, 1)

            pe.wait_ge(consts, 3)
            pe.wait_ge(small_in, 16 * 10)
            tr(PS[0][:, 0:P], rows_in[:], ident[:]).then_inc(cols_ps, 1)
            with pe.Fori(0, ADA_FIRST // 2) as j:
                for u in range(2):
                    pe.wait_ge(ada_sum, j * 2 + (u + 1))
                    if u == 1:
                        pe.wait_ge(ada_rowok, j * 2 + 1)
                    mm(PS[2 + u][0:1, 0:ADA_W], ones[:, 0:1], ada_acc[:, u, :], start=True, stop=True).then_inc(ada_ps, 1)
            pe.wait_ge(ada_rowok, ADA_FIRST)
            norm_transposes(0)
            hT_ready(0)
            pe.wait_ge(small2_in, 16 * 10)
            narrow(abW, 2 * H, decay_ps)
            pe.wait_ge(decay_dve, 2)
            mm(PS[5][:, 0:32], upto[:], la, start=True, stop=True)
            mm(PS[5][:, 32:64], ones[:], la, start=True, stop=True).then_inc(decay_ps, 1)

            def project(s, w_n, slot, a, b):
                for f in range(a, b):
                    m, k = f // KD, f % KD
                    if f == 0:
                        pe.wait_ge(gdn_w[slot], w_n * 64)
                    if k == 0:
                        n = s * 4 + (m - 1)
                        after(pe, ev_pj, n)
                    last = mm(PS[m % 2][:], Wr[:, slot, k, m * P:m * P + P], hT[:, k, :],
                              start=(k == 0), stop=(k == KD - 1))
                    if k == KD - 1:
                        last.then_inc(proj_ps, 1)

            def ada_item(d, q, par):
                pe.wait_ge(ada_sum2, d * 5 + (q + 1))
                if q == 0:
                    pe.wait_ge(kd_ok, d + 1)
                else:
                    pe.wait_ge(ada_rowok, d * 5 + (ADA_FIRST + q))
                mm(PS[2][0:1, 0:ADA_W], ones[:, 0:1], ada_acc[:, (par + q) % 2, :], start=True, stop=True).then_inc(ada_ps, 1)

            def delta(d, fill, par):
                pe.wait_ge(row_ok, d + 1)
                after(pe, ada_rowok, d * 5 + ADA_FIRST)
                after(pe, ro_ok, d)
                for n in range(NT):
                    mm(tile(PS[2], n), lah[:, 0, n:n + 1].to_broadcast([P, P]), upto[:], start=True, stop=True)
                for n in range(NT):
                    last = mm(tile(PS[3], n), lah[:, 1, n:n + 1].to_broadcast([P, P]), ident[:], start=True, stop=True)
                last.then_inc(gb_ps, 1)
                fill(0, 4)
                pe.wait_ge(sq_ok, d + 1)
                mm(PS[4][:], ones[:], sqk, start=True, stop=True).then_inc(ss_ps, 1)
                mm(PS[5][:], ones[:], sqq, start=True, stop=True).then_inc(ss_ps, 1)
                after(pe, s_ok, d * 3)
                for n in range(NT):
                    last = tr(tile(PS[6], n), tile(qkv[2], n), ident[:])
                last.then_inc(v_ps, 1)
                fill(4, 6)
                pe.wait_ge(hat_ok, d + 1)
                pe.wait_ge(egb_ok, d + 1)
                for n in range(NT):
                    last = tr(tile(PS[2], n), tile(khat, n), ident[:])
                last.then_inc(k_ps, 1)
                fill(6, 7)
                pe.wait_ge(kb_ok, d + 1)
                for n in range(NT):
                    last = mm(tile(PS[3], n), tile(khat, n), tile(kb, n), start=True, stop=True)
                last.then_inc(kk_ps, 1)
                for n in range(NT):
                    last = mm(tile(PS[4], n), tile(khat, n), tile(qhat, n), start=True, stop=True)
                last.then_inc(qk_ps, 1)
                fill(7, 10)
                pe.wait_ge(xt_ok, d + 1)
                for n in range(NT):
                    last = tr(tile(PS[5], n), tile(XiT, n), ident[:])
                last.then_inc(x1_ps, 1)
                fill(10, 12)
                for l in range(1, LEVELS):
                    if l == 1:
                        pe.wait_ge(x1_ok, d + 1)
                        pe.wait_ge(qkt_ok, d + 1)
                    else:
                        pe.wait_ge(lv_ok, d * 6 + (l - 1))
                    pe.wait_ge(nt_ok, d * 6 + l)
                    for n in range(NT):
                        last = mm(tile(PS[4], n), tile(nt[l], n), tile(Xi, n), start=True, stop=True)
                    last.then_inc(p_ps, 1)
                    fill(10 + 2 * l, 11 + 2 * l)
                    if l % 2:
                        ada_item(d, l // 2, par)
                    pe.wait_ge(p_ok, d * 6 + l)
                    if l < LEVELS - 1:
                        for n in range(NT):
                            mm(tile(PS[5], n), tile(XiT, n), tile(Pp, n), start=True, stop=True)
                    for n in range(NT):
                        last = mm(tile(PS[6], n), tile(Pp, n), tile(XiT, n), start=True, stop=True)
                    last.then_inc(lv_ps, 1)
                    fill(11 + 2 * l, 12 + 2 * l)
                pe.wait_ge(lv_ok, d * 6 + 6)
                for n in range(NT):
                    last = mm(tile(PS[4], n), tile(kwn, n), tile(XiT, n), start=True, stop=True)
                last.then_inc(wt_ps, 1)
                fill(24, 25)
                for n in range(NT):
                    last = mm(PS[5][:, 0:P], tile(XiT, n), tile(vb, n), start=True, stop=(n == 0))
                    if n > 0:
                        if n == 1:
                            pe.wait_ge(wt_ok, d + 1)
                        pe.wait_ge(s_ok, d * 3 + n)
                        last = mm(PS[5][:, 0:P], tile(nWT, n), S, start=False, stop=True)
                    last.then_inc(vn_ps, 1)
                    if n == 2:
                        ada_item(d, 3, par)
                    fill(25 + n, 26 + n)
                    if n == 0:
                        after(pe, ot_ok, d)
                        pe.wait_ge(qg_ok, d + 1)
                    else:
                        mm(tile(PS[7], n), S, tile(qg, n), start=True, stop=False)
                    pe.wait_ge(vn_ok, d * 4 + (n + 1))
                    last = mm(tile(PS[7], n), vnew[:, n % 2, :], tile(qkT, n), start=(n == 0), stop=True)
                    if n < NT - 1:
                        last = mm(PS[6][:, 0:P], tile(kdec_k, n), vnew[:, n % 2, :], start=True, stop=True)
                        last.then_inc(s_ps, 1)
                    else:
                        last.then_inc(o_ps, 1)
                ada_item(d, 4, par)
                fill(29, 31)
                pe.wait_ge(osq_ok, d + 1)
                mm(PS[3][:], ones[:], osq, start=True, stop=True).then_inc(sso_ps, 1)
                fill(31, 32)

            def no_fill(a, b):
                pass

            project(0, 1, 0, 0, 32)

            def step(s, w_n, slot):
                delta(s - 1, lambda a, b: project(s, w_n, slot, a, b), 1 - slot)

            step(1, 1, 1)
            with pe.Fori(0, 3) as j:
                step(j * 2 + 2, j + 2, 0)
                step(j * 2 + 3, j + 2, 1)
            delta(H - 1, no_fill, 1)
            pe.wait_ge(ada_rowok, ADA_FIRST + ADA_PER_HEAD * H)

            def out_projection(layer, w_sem, ready, ready_n):
                pe.wait_ge(ready, ready_n)
                for nh in range(2):
                    pe.wait_ge(w_sem[nh], 64 * 4 + 16)
                    for n in range(NT):
                        u = nh * NT + n
                        base = layer * (2 * NT + 1)
                        if u >= 2:
                            pe.wait_ge(wo_ok, base + u - 1)
                        elif layer == 0:
                            pe.wait_ge(ev_pj, 4 * H)
                        else:
                            pe.wait_ge(fev, 4 * H)
                        for k in range(KD):
                            last = mm(PS[u % 2][:], tile(OT[:, k, :], n), Wr[:, nh, k, :], start=(k == 0), stop=(k == KD - 1))
                        last.then_inc(wo_ps, 1)

            def experts(i):
                m = M
                B = i * NE
                base = i * (2 * NT + 1)
                pe.wait_ge(wo_ok, base + 2 * NT)
                norm_transposes(2 * i + 1)
                hT_ready(2 * i + 1)
                narrow(routW[:, i], NG + NE, r_ps)
                pe.wait_ge(r_both, i + 1)
                for n in range(NT):
                    for a in range(n + 1):
                        mm(PS[5][:, n * NE:(n + 1) * NE], (before if a == n else ones)[:], both[:, a, :],
                           start=(a == 0), stop=(a == n))
                for a in range(NT):
                    last = mm(PS[5][:, NT * NE:(NT + 1) * NE], ones[:], both[:, a, :], start=(a == 0), stop=(a == NT - 1))
                last.then_inc(r_rank, 1)
                for b in range(NT):
                    pe.wait_ge(r_pos, NT * i + b + 1)
                    place = place1 if b % 2 == 0 else place2
                    for u in range(2 * NT):
                        last = mm(PS[4][:, b * NE:(b + 1) * NE], place[:, u, :], ohd[u // NT][:, u % NT, :],
                                  start=(u == 0), stop=(u == 2 * NT - 1))
                    last.then_inc(slots_ps, 1)

                def turn(u, n_in):
                    pe.wait_ge(m["xg"][u], n_in + 4 * B)
                    for k in range(KD):
                        last = tr(PS[2 + k // 4][:, (k % 4) * P:(k % 4) * P + P], xg[u][:, k * P:k * P + P], ident[:])
                    last.then_inc(m["xt_ps"], 1)

                def gate_up(e, u, slot, w_n):
                    pe.wait_ge(m["xt_a"], e + (B + 1))
                    pe.wait_ge(m["xt_b"], e + (B + 1))
                    pe.wait_ge(moe_w[slot], w_n * 16 + 4 * B)
                    for k in range(KD):
                        last = mm(PS[u][:], xgT[u][:, k, :], Wr[:, slot, k, :], start=(k == 0), stop=(k == KD - 1))
                    last.then_inc(m["gu_ps"], 1)

                def turn_act(e, u):
                    pe.wait_ge(m["ac"], e + (B + 1))
                    for k in range(2):
                        last = tr(tile(PS[4], k), ac[u][:, k * P:k * P + P], ident[:])
                    last.then_inc(m["at_ps"], 1)

                def down(e, u, w_n):
                    pe.wait_ge(m["at"], e + (B + 1))
                    pe.wait_ge(moe_d[u], w_n * 16 + 8 * B)
                    if not isinstance(e, int) or e > 0:
                        pe.wait_ge(m["ya"], e + B)
                        pe.wait_ge(m["yb"], e + B)
                    for nh in range(2):
                        for k in range(2):
                            last = mm(PS[6 + nh][:], acT[u][:, k, :],
                                      Dr[:, u, k * D + nh * 512:k * D + nh * 512 + 512], start=(k == 0), stop=(k == 1))
                    last.then_inc(m["dn_ps"], 1)

                turn(0, 16)
                gate_up(0, 0, 2, 1)
                pe.wait_ge(m["xt_a"], B + 1)
                turn(1, 16)

                def step(e, q, w_n, d_n, x_n, rows=True):
                    gate_up(e, q % 2, (q + 2) % 4, w_n)
                    turn_act(e - 1, (q + 1) % 2)
                    if rows:
                        turn((q + 1) % 4, x_n)
                    down(e - 1, (q + 1) % 2, d_n)

                for e in range(1, 5):
                    step(e, e % 4, e // 4 + 1, (e - 1) // 2 + 1, 16 * ((e + 1) // 4 + 1))
                with pe.Fori(0, 6) as j:
                    for q in range(4):
                        e0 = 5 + q
                        step(j * 4 + e0, e0 % 4, j + (e0 // 4 + 1), j * 2 + ((e0 - 1) // 2 + 1),
                             (j + ((e0 + 1) // 4 + 1)) * 16)
                for e in range(29, NE):
                    step(e, e % 4, e // 4 + 1, (e - 1) // 2 + 1, 16 * ((e + 1) // 4 + 1), rows=(e < NE - 1))
                turn_act(NE - 1, 1)
                down(NE - 1, 1, NE // 2)

                xm = MX[i]
                pe.wait_ge(idx_ok, 2 * i + 2)
                n_x = pe.value_load(nextra[0:1, 0:1], min_val=0, max_val=MORE)
                pe.wait_ge(m["ya"], B + NE)
                pe.wait_ge(m["yb"], B + NE)
                with pe.If(n_x > 0):
                    with pe.Fori(0, n_x) as j:
                        pe.wait_ge(xm["moved"], j * 32 + 16)
                        for k in range(KD):
                            last = tr(PS[2 + k // 4][:, (k % 4) * P:(k % 4) * P + P], xg[0][:, k * P:k * P + P], ident[:])
                        last.then_inc(xm["stage"], 1)
                        pe.wait_ge(xm["stage"], stage_n("xt", j))
                        pe.wait_ge(xm["w"], (j + 1) * 32)
                        for k in range(KD):
                            last = mm(PS[0][:], xgT[0][:, k, :], Wr[:, 2, k, :], start=(k == 0), stop=(k == KD - 1))
                        last.then_inc(xm["stage"], 1)
                        pe.wait_ge(xm["stage"], stage_n("ac", j))
                        for k in range(2):
                            last = tr(tile(PS[4], k), ac[0][:, k * P:k * P + P], ident[:])
                        last.then_inc(xm["stage"], 1)
                        pe.wait_ge(xm["stage"], stage_n("at", j))
                        for nh in range(2):
                            for k in range(2):
                                last = mm(PS[6 + nh][:], acT[0][:, k, :],
                                          Dr[:, 0, k * D + nh * 512:k * D + nh * 512 + 512], start=(k == 0), stop=(k == 1))
                        last.then_inc(xm["stage"], 1)
                with pe.Else():
                    pe.nop()
                pe.nop()

            out_projection(0, gdn_w, ot_ok, H)
            experts(0)

            pe.wait_ge(wo_ok, 2 * NT + 1)
            norm_transposes(2)
            hT_ready(2)
            narrow(fW, 2 * H, forget_ps)
            pe.wait_ge(forget_dve, 2)
            w16 = 2 * H
            mm(PS[5][:, 0:NT * w16], upto[:], lf, start=True, stop=False)
            for a in range(NT - 1):
                for n in range(a + 1, NT):
                    last = mm(PS[5][:, n * w16:(n + 1) * w16], ones[:], lf[:, a * w16:(a + 1) * w16],
                              start=False, stop=(a == NT - 2))
            last.then_inc(forget_ps, 1)

            def project_pair(p, w_n, slot, a, b):
                for f in range(a, b):
                    if f == 0:
                        pe.wait_ge(fox_w[slot], w_n * 64)
                    if f < 16:
                        m, k = f // KD, f % KD
                        if k == 0:
                            after(pe, fev, p * 4 + (m - 1))
                        last = mm(PS[m][:], Wr[:, slot, k, m * P:m * P + P], hT[:, k, :], start=(k == 0), stop=(k == KD - 1))
                        if k == KD - 1:
                            last.then_inc(fpj_ps, 1)
                    else:
                        n, k = (f - 16) // KD, f % KD
                        if k == 0 and n % 2 == 0:
                            after(pe, fev, p * 4 + (n // 2 + 1))
                        last = mm(PS[n // 2][:, (n % 2) * 256:(n % 2) * 256 + 256], tile(hT[:, k, :], n),
                                  Wr[:, slot, k, 256:512], start=(k == 0), stop=(k == KD - 1))
                        if k == KD - 1 and n % 2 == 1:
                            last.then_inc(fpj_ps, 1)

            def attend(p, fill):
                fill(0, 3)
                pe.wait_ge(fev, p * 4 + 4)
                after(pe, ont_ok, p)
                after(pe, on_ok, p)
                mm(PS[7][:], halves[:], sqr[0], start=True, stop=True).then_inc(fs_ps, 1)
                mm(PS[6][:], halves[:], sqr[1], start=True, stop=True).then_inc(fs_ps, 1)
                fill(3, 4)
                for a in range(2):
                    if a == 0:
                        pe.wait_ge(nch_ok, p + 1)
                        pe.wait_ge(fr_ok, p * 2 + 1)
                    else:
                        pe.wait_ge(cb_ok, p * 2 + 1)
                    for n in range(NT):
                        last = mm(tile(PS[7], n), nch[:, a, n:n + 1].to_broadcast([P, P]), ident[:], start=True, stop=True)
                    last.then_inc(cb_ps, 1)
                    fill(4 + a, 5 + a)
                pe.wait_ge(qkh_ok, p * 2 + 2)

                def scores(u):
                    a, qt = u // NT, u % NT
                    w = (qt + 1) * P
                    after(pe, sc_ok, p * 8 + (u - 1))
                    mm(PS[2 + u % 2][:, 0:w], tile(qh, qt)[64 * a:64 * a + 64, :], kh[64 * a:64 * a + 64, 0:w],
                       start=True, stop=True).then_inc(sc_ps, 1)

                scores(0)
                for u in range(8):
                    a, qt = u // NT, u % NT
                    if u < 7:
                        scores(u + 1)
                    fill(6 + 4 * u, 8 + 4 * u)
                    pe.wait_ge(pr_ok, p * 8 + (u + 1))
                    n_free = p * 8 + (u - 1)
                    after(pe, pt_ok, n_free)
                    for n in range(qt + 1):
                        last = tr(tile(PS[4 + u % 2], n), tile(pS[u % 2], n), ident[:])
                    last.then_inc(pt_ps, 1)
                    fill(8 + 4 * u, 10 + 4 * u)
                    pe.wait_ge(pt_ok, p * 8 + (u + 1))
                    if u == 0:
                        pe.wait_ge(vs_ok, p + 1)
                        pe.wait_ge(fr_ok, p * 2 + 2)
                    for n in range(qt + 1):
                        last = mm(PS[6][:, qt * P + 64 * a:qt * P + 64 * a + 64], tile(pT[u % 2], n),
                                  vS[:, n, 64 * a:64 * a + 64], start=(n == 0), stop=(n == qt))
                    last.then_inc(pv_ps, 1)
                fill(38, 48)
                pe.wait_ge(on_ok, p + 1)
                for n in range(NT):
                    last = tr(tile(PS[7], n), on[:, n, :], ident[:])
                last.then_inc(ont_ps, 1)

            project_pair(0, 1, 0, 0, 48)

            def pair_step(s, w_n, slot):
                attend(s - 1, lambda a, b: project_pair(s, w_n, slot, a, b))

            pair_step(1, 1, 1)
            with pe.Fori(0, 3) as j:
                pair_step(j * 2 + 2, j + 2, 0)
                pair_step(j * 2 + 3, j + 2, 1)
            attend(7, no_fill)

            out_projection(1, fox_w, ont_ok, H)
            experts(1)

        @block.scalar
        def _(act):
            A = nc.scalar.activation
            link = Link(act, act_link)
            eps_ap, one_ap = eps_c[:, 0:1], eps_c[:, 1:2]

            def cp(dst, src):
                return nc.scalar.copy(dst, src)

            def rsqrt(dst, src, scale, bias, tmp=None):
                tmp = dst if tmp is None else tmp
                link(A(tmp, src, ACT.Ln, bias=eps_ap[0:dst.shape[0]], scale=scale))
                return A(dst, tmp, ACT.Exp, bias=bias, scale=-0.5)

            def norm(phase):
                for n in range(NT):
                    if phase == 0 and n == 0:
                        act.wait_ge(x_in, 16)
                    link(A(sq_junk, X[:, n, :], ACT.Square, accum_out=ss[:, n:n + 1]))
                rsqrt(rstd[:], ss[:], 1.0 / D, 0.0).then_inc(n_rs, 1)
                if phase < 4:
                    for n in range(NT):
                        act.wait_ge(n_tr, 4 * phase + n + 1)
                        cp(hT[:, 0:4, n * P:n * P + P], PS[2 * (n % 2)][:].rearrange("p (k j) -> p k j", k=4)).then_inc(n_ta, 1)

            act.wait_ge(consts, 4)
            act.wait_ge(small_in, 16 * 10)
            link(A(nega[:], nega[:], ACT.Exp))
            nc.scalar.mul(nega[:], nega[:], -1.0).then_inc(act_setup, 1)
            act.wait_ge(cols_ok, 1)
            A(cact[:], cols[:, 96:104], ACT.Silu).then_inc(act_setup, 1)
            with act.Fori(0, ADA_FIRST // 2) as j:
                for u in range(2):
                    act.wait_ge(ada_ps, j * 2 + (u + 1))
                    cp(ada_row[:, u, :], PS[2 + u][0:1, 0:ADA_W]).then_inc(ada_rowok, 1)
                    act.wait_ge(ada_rowok, j * 2 + (u + 1))
                    act.dma_start(ada_rows[0:1, ds((j * 2 + u) * ADA_W, ADA_W)], ada_row[:, u, :]).then_inc(ada_out[u], 16)
                    act.wait_ge(ada_out[u], (j + 1) * 16)
            norm(0)

            act.wait_ge(decay_dve, 1)
            link(A(t_ab2, t_ab2, ACT.Exp))
            link(A(t_ab2, t_ab2, ACT.Ln, bias=one_ap))
            A(beta, beta, ACT.Exp, scale=-1.0).then_inc(decay_act, 1)
            act.wait_ge(decay_dve, 3)
            link(A(nbeg, gc, ACT.Exp))
            link(A(kdecay, kdecay, ACT.Exp))
            A(egl, egl, ACT.Exp).then_inc(decay_act, 1)

            def take_product(s, m):
                act.wait_ge(proj_ps, s * 4 + (m + 1))
                if m == 2:
                    act.wait_ge(conv_ok, s * 3 + 1)
                else:
                    after(act, conv_ok, s * 3 + (-1 if m == 1 else 0))
                cp(cin[m % 2][:, CONV - 1:], PS[m % 2][:]).then_inc(ev_pj, 1)

            def squares(s):
                A(sqk, qkv[1], ACT.Square)
                A(sqq, qkv[0], ACT.Square).then_inc(sq_ok, 1)

            def delta(d, take, par):
                act.wait_ge(ss_ps, d * 2 + 1)
                rsqrt(sqk, PS[4][:], 1.0, 0.0).then_inc(rr_ok, 1)
                act.wait_ge(ss_ps, d * 2 + 2)
                rsqrt(sqq, PS[5][:], 1.0, eps_c[:, 2:3]).then_inc(rr_ok, 1)
                act.wait_ge(diff_ok, d + 1)
                A(egB, PS[2][:], ACT.Exp).then_inc(egb_ok, 1)
                act.wait_ge(msk_ok, d + 1)
                A(dT, dT, ACT.Exp).then_inc(dT_ok, 1)
                take(0)
                act.wait_ge(x1_ps, d + 1)
                cp(Xi, PS[5][:]).then_inc(x1_ok, 1)
                for l in range(1, LEVELS):
                    act.wait_ge(p_ps, d * 6 + l)
                    cp(Pp, PS[4][:]).then_inc(p_ok, 1)
                    if l == 2:
                        take(1)
                    if l % 2:
                        ada_item(d, l // 2, par)
                take(2)
                act.wait_ge(wt_ps, d + 1)
                cp(nWT, PS[4][:]).then_inc(wt_ok, 1)
                for n in range(NT):
                    act.wait_ge(vn_ps, d * 4 + (n + 1))
                    cp(vnew[:, n % 2, :], PS[5][:, 0:P]).then_inc(vn_ok, 1)
                    if n == 2:
                        ada_item(d, 3, par)
                act.wait_ge(o_ps, d + 1)
                A(osq, PS[7][:], ACT.Square).then_inc(osq_ok, 1)
                ada_item(d, 4, par)
                act.wait_ge(sso_ps, d + 1)
                rsqrt(rB, PS[3][:], 1.0 / P, 0.0).then_inc(ro_ok, 1)

            def ada_item(d, q, par):
                slot = (par + q) % 2
                act.wait_ge(ada_ps, d * 5 + (ADA_FIRST + q + 1))
                act.wait_ge(ada_out[slot], ada_stored(d, q, par))
                cp(ada_row[:, slot, :], PS[2][0:1, 0:ADA_W]).then_inc(ada_rowok, 1)
                act.wait_ge(ada_rowok, d * 5 + (ADA_FIRST + q + 1))
                layer, col = (0, (d * 2 + 8 + q) * ADA_W) if q < 2 else (1, (d * 3 + (q - 2)) * ADA_W)
                act.dma_start(ada_rows[layer:layer + 1, ds(col, ADA_W)], ada_row[:, slot, :]).then_inc(ada_out[slot], 16)

            def ada_stored(d, q, par):
                if isinstance(d, int):
                    n = ADA_FIRST + 5 * d + q
                    return 16 * (n // 2)
                return (d * 5 + (ADA_FIRST + q - (par + q) % 2)) * 8

            def step(s, slot):
                take = lambda m: take_product(s, m)
                delta(s - 1, take, (slot + 1) % 2)
                end_of_step(s)

            def end_of_step(s):
                act.wait_ge(proj_ps, s * 4 + 4)
                after(act, ot_ok, s)
                A(gate_s, PS[1][:], ACT.Silu).then_inc(ev_pj, 1)
                act.wait_ge(conv_ok, s * 3 + 3)
                for m in range(3):
                    ins = A(qkv[m], qkv[m], ACT.Silu)
                link(ins)
                squares(s)

            for m in range(3):
                take_product(0, m)
            end_of_step(0)
            step(1, 1)
            with act.Fori(0, 3) as j:
                link.enter(j, 8)
                step(j * 2 + 2, 0)
                step(j * 2 + 3, 1)
                link.leave(3)
            delta(7, lambda m: None, 1)

            def experts(i):
                m = M
                B = i * NE
                act.wait_ge(wo_ok, i * (2 * NT + 1) + 2 * NT)
                norm(2 * i + 1)
                act.wait_ge(r_m, i + 1)
                link(A(gidx, gidx, ACT.Exp))
                A(e21, e21, ACT.Exp).then_inc(r_e, 1)

                def rows(e, u):
                    act.wait_ge(m["xt_ps"], e + (B + 1))
                    if not isinstance(e, int) or e >= 2:
                        act.wait_ge(m["gu_ps"], e + (B - 1))
                    cp(xgT[u][:, 0:4, :], PS[2][:].rearrange("p (k j) -> p k j", k=4)).then_inc(m["xt_a"], 1)

                def silu(e, u):
                    act.wait_ge(m["gu_ps"], e + (B + 1))
                    if not isinstance(e, int) or e >= 2:
                        act.wait_ge(m["ac"], e + (B - 1))
                    A(sg[u], PS[u][:, 0:DE], ACT.Silu).then_inc(m["sg"], 1)

                def act_turned(e, u):
                    act.wait_ge(m["at_ps"], e + (B + 1))
                    if not isinstance(e, int) or e >= 2:
                        act.wait_ge(m["dn_ps"], e + (B - 1))
                    cp(acT[u], PS[4][:, 0:2 * P].rearrange("p (k j) -> p k j", k=2)).then_inc(m["at"], 1)

                def result(e, u, y_n):
                    act.wait_ge(m["dn_ps"], e + (B + 1))
                    if y_n is not None:
                        act.wait_ge(m["y"][u], y_n + 8 * B)
                    cp(yo[u][:, 0:512], PS[6][:]).then_inc(m["ya"], 1)

                rows(0, 0)
                rows(1, 1)

                def step(e, q, y_n, more=True):
                    silu(e, q % 2)
                    if not isinstance(e, int) or e >= 1:
                        act_turned(e - 1, (q + 1) % 2)
                        if more:
                            rows(e + 1, (q + 1) % 2)
                        result(e - 1, (q + 1) % 2, y_n)

                def y_free(e):
                    n = (e - 1) // 2
                    return 16 * n if n > 0 else None

                for e in range(0, 5):
                    step(e, e % 4, y_free(e) if e else None)
                with act.Fori(0, 6) as j:
                    for q in range(4):
                        e0 = 5 + q
                        step(j * 4 + e0, e0 % 4, (j * 2 + (e0 - 1) // 2) * 16)
                for e in range(29, NE):
                    step(e, e % 4, y_free(e), more=(e < NE - 1))
                act_turned(NE - 1, 1)
                result(NE - 1, 1, 16 * (NE // 2 - 1))

                xm = MX[i]
                act.wait_ge(idx_ok, 2 * i + 2)
                n_x = act.value_load(nextra[0:1, 0:1], min_val=0, max_val=MORE)
                with act.If(n_x > 0):
                    with act.Fori(0, n_x) as j:
                        act.wait_ge(xm["stage"], stage_n("gu_ps", j))
                        A(sg[0], PS[0][:, 0:DE], ACT.Silu).then_inc(xm["stage"], 1)
                        act.wait_ge(xm["stage"], stage_n("at_ps", j))
                        cp(acT[0], PS[4][:, 0:2 * P].rearrange("p (k j) -> p k j", k=2)).then_inc(xm["stage"], 1)
                with act.Else():
                    act.nop()
                act.nop()

            experts(0)

            act.wait_ge(wo_ok, 2 * NT + 1)
            norm(2)
            act.wait_ge(forget_dve, 1)
            link(A(tf2, tf2, ACT.Exp))
            A(tf2, tf2, ACT.Ln, bias=one_ap).then_inc(forget_act, 1)

            def take_pair(p, m):
                act.wait_ge(fpj_ps, p * 4 + (m + 1))
                if m < 2:
                    if m == 0:
                        after(act, qkh_ok, p * 2)
                    A(sqr[m], PS[m][:], ACT.Square)
                    ins = cp(qkr[m], PS[m][:])
                else:
                    ap = PS[m - 2][:].rearrange("p (n c) -> p n c", n=2)
                    lo = 2 * (m - 2)
                    if m == 2:
                        after(act, vs_ok, p)
                        after(act, sgt_ok, p)
                    cp(vraw[:, lo:lo + 2, :], ap[:, :, 0:P])
                    ins = A(eg[:, lo:lo + 2, :], ap[:, :, P:2 * P], ACT.Exp, scale=-1.0)
                ins.then_inc(fev, 1)

            def attend(p, take):
                act.wait_ge(fs_ps, p * 2 + 1)
                rsqrt(sqr[0], PS[7][:], 1.0 / 64, eps_c[:, 3:4]).then_inc(fr_ok, 1)
                act.wait_ge(fs_ps, p * 2 + 2)
                rsqrt(sqr[1], PS[6][:], 1.0 / 64, 0.0).then_inc(fr_ok, 1)
                for a in range(2):
                    act.wait_ge(cb_ps, p * 2 + (a + 1))
                    if a == 0:
                        after(act, cbt_ok, p * 2)
                    cp(cbS[:, a, :], PS[7][:]).then_inc(cb_ok, 1)
                for u in range(8):
                    qt = u % NT
                    w = (qt + 1) * P
                    act.wait_ge(sc_ok, p * 8 + (u + 1))
                    if u == 0:
                        after(act, on_ok, p)
                    n_free = p * 8 + (u - 1)
                    after(act, pt_ps, n_free)
                    A(pS[u % 2][:, 0:w], sS[u % 2][:, 0:w], ACT.Exp, bias=nmx[:, u:u + 1],
                      accum_out=rsum[:, u:u + 1]).then_inc(pr_ok, 1)
                    act.wait_ge(pt_ps, p * 8 + (u + 1))
                    after(act, pv_ps, n_free)
                    cp(pT[u % 2][:, 0:w], PS[4 + u % 2][:, 0:w]).then_inc(pt_ok, 1)
                    if u == 1:
                        take(0)
                    if u == 3:
                        take(1)
                    if u == 7:
                        take(2)
                act.wait_ge(ont_ps, p + 1)
                cp(OT[:, ds(p, 1), :].rearrange("p a t -> p (a t)"), PS[7][:]).then_inc(ont_ok, 1)
                take(3)

            for m in range(4):
                take_pair(0, m)

            def pair_step(s):
                attend(s - 1, lambda m: take_pair(s, m))

            pair_step(1)
            with act.Fori(0, 3) as j:
                link.enter(j, 4)
                pair_step(j * 2 + 2)
                pair_step(j * 2 + 3)
                link.leave(3)
            attend(7, lambda m: None)
            experts(1)
            act.wait_ge(wo_ok, 2 * (2 * NT + 1))
            norm(4)

        @block.vector
        def _(dve):
            TT, TS, STT = nc.vector.tensor_tensor, nc.vector.tensor_scalar, nc.vector.scalar_tensor_tensor
            link = Link(dve, dve_link)
            cpv = nc.vector.tensor_copy

            dve.wait_ge(consts, 4)
            xi = hT[:, 0, 0:P].bitcast(I32)
            xj = hT[:, 0, P:2 * P].bitcast(I32)
            xl = hT[:, 1, 0:P].bitcast(I32)
            xf = hT[:, 2, 0:P]
            link(TT(xi, xi, xj, ALU.bitwise_xor))
            for l in range(LEVELS):
                link(TS(xl, xi, l, None, ALU.logical_shift_right))
                link(TS(xf, xl, 1.0, -1.0, ALU.is_equal, ALU.mult))
                link(TT(negmask[:, l, :], xf, before[:], ALU.mult))
            dve.wait_ge(cols_ps, 1)
            cpv(cols[:], PS[0][:, 0:P]).then_inc(cols_ok, 1)
            dve.wait_ge(act_setup, 2)

            with dve.Fori(0, ADA_FIRST // 2) as j:
                link.enter(j, 2 * (KD - 1))
                for u in range(2):
                    dve.wait_ge(ada_in[u], (j + 1) * 32)
                    if u == 1:
                        dve.wait_ge(ada_ps, j * 2 + 1)
                    w = Dr[:, u, :].rearrange("p (k n) -> p k n", k=KD)
                    for k in range(KD):
                        ins = STT(out=ada_acc[:, u, :], in0=w[:, k, :], scalar=cact[:, k:k + 1],
                                  in1=bias_row[:, u, :] if k == 0 else ada_acc[:, u, :], op0=ALU.mult, op1=ALU.add)
                        if k < KD - 1:
                            link(ins)
                    ins.then_inc(ada_sum, 1)
                    dve.wait_ge(ada_ps, j * 2 + (u + 1))
                link.leave(ADA_FIRST // 2)

            def norm(phase):
                dve.wait_ge(bc_in, 32 * (phase + 1))
                link(TS(scaleB[:], scaleB[:], 1.0, None, ALU.add))
                dve.wait_ge(n_rs, phase + 1)
                for n in range(NT):
                    if n >= 2:
                        dve.wait_ge(n_tr, 4 * phase + n - 1)
                        if phase % 2:
                            dve.wait_ge(hr_out[n % 2], 16 * (2 * (phase // 2) + n // 2))
                    link(STT(out=hrow[n % 2], in0=X[:, n, :], scalar=rstd[:, n:n + 1], in1=scaleB[:], op0=ALU.mult, op1=ALU.mult))
                    TT(hrow[n % 2], hrow[n % 2], shiftB[:], ALU.add).then_inc(n_h, 1)
                    if n >= 1:
                        take_tile(phase, n - 1)
                take_tile(phase, NT - 1)

            def take_tile(phase, n):
                dve.wait_ge(n_tr, 4 * phase + n + 1)
                cpv(hT[:, 4:8, n * P:n * P + P], PS[2 * (n % 2) + 1][:].rearrange("p (k j) -> p k j", k=4)).then_inc(n_tb, 1)

            norm(0)

            hn = lambda ap: ap.rearrange("p (h n) -> p n h", h=H)
            dve.wait_ge(decay_ps, 1)
            ab = PS[4][:, 0:NT * 2 * H].rearrange("p (n c) -> p n c", n=NT)
            link(TT(hn(t_ab), ab[:, :, 0:H], dtb[:].unsqueeze(1).to_broadcast([P, NT, H]), ALU.add))
            link(TS(t_ab2, t_ab, -1.0, None, ALU.mult))
            TT(t_ab2, t_ab2, t_ab, ALU.min)
            cpv(hn(beta), ab[:, :, H:2 * H]).then_inc(decay_dve, 1)
            dve.wait_ge(decay_act, 1)
            link(STT(out=la, in0=t_ab, scalar=0.0, in1=t_ab2, op0=ALU.max, op1=ALU.add))
            dve.wait_ge(act_setup, 1)
            link(TT(hn(la), hn(la), nega[:].unsqueeze(1).to_broadcast([P, NT, H]), ALU.mult))
            link(TS(beta, beta, 1.0, None, ALU.add))
            nc.vector.reciprocal(beta, beta).then_inc(decay_dve, 1)
            dve.wait_ge(decay_ps, 2)
            link(cpv(gc, PS[5][:, 0:32]))
            link(cpv(egl, PS[5][:, 32:64]))
            TT(kdecay, egl, gc, ALU.subtract).then_inc(decay_dve, 1)
            dve.wait_ge(decay_act, 2)
            STT(out=nbeg, in0=nbeg, scalar=-1.0, in1=beta, op0=ALU.mult, op1=ALU.mult).then_inc(decay_dve, 1)
            dve.wait_ge(decay_dve, 4)

            def hcol(ap, d):
                return over(ap[:, ds(d * NT, NT)])

            def conv(s, m):
                dve.wait_ge(row_ok, s + 1)
                dve.wait_ge(ev_pj, s * 4 + (m + 1))
                src = cin[m % 2]
                for j in range(CONV):
                    tap = taps[:, j * 3 + m:j * 3 + m + 1]
                    if j == 0:
                        link(TS(qkv[m], src[:, 0:T], tap, None, ALU.mult))
                    else:
                        ins = STT(out=qkv[m], in0=src[:, j:j + T], scalar=tap, in1=qkv[m], op0=ALU.mult, op1=ALU.add)
                        if j < CONV - 1:
                            link(ins)
                ins.then_inc(conv_ok, 1)

            def delta(d, s):
                after(dve, ot_ok, d)
                dve.wait_ge(gb_ps, d + 1)
                TT(t4(dT), t4(PS[2][:]), hcol(gc, d), ALU.subtract).then_inc(diff_ok, 1)
                dve.wait_ge(rr_ok, d * 2 + 1)
                TT(khat, qkv[1], sqk, ALU.mult)
                dve.wait_ge(rr_ok, d * 2 + 2)
                TT(qhat, qkv[0], sqq, ALU.mult).then_inc(hat_ok, 1)
                dve.wait_ge(hat_ok, d + 1)
                TT(kb, khat, PS[3][:], ALU.mult).then_inc(kb_ok, 1)
                dve.wait_ge(egb_ok, d + 1)
                TT(qg, qhat, egB, ALU.mult).then_inc(qg_ok, 1)
                dve.wait_ge(v_ps, d + 1)
                TT(t4(vb), t4(PS[6][:]), hcol(beta, d), ALU.mult).then_inc(vb_ok, 1)
                dve.wait_ge(k_ps, d + 1)
                TT(t4(kwn), t4(PS[2][:]), hcol(nbeg, d), ALU.mult)
                TT(t4(kdec_k), t4(PS[2][:]), hcol(kdecay, d), ALU.mult).then_inc(kd_ok, 1)
                dve.wait_ge(kk_ps, d + 1)
                dve.wait_ge(dT_ok, d + 1)
                TT(aT, PS[3][:], dT, ALU.mult).then_inc(at_ok, 1)
                dve.wait_ge(at_ok, d + 1)
                link(TT(t4(nt[0]), t4(aT), negmask[:, 0:1, :].to_broadcast([P, NT, P]), ALU.mult))
                TT(t4(XiT), t4(nt[0]), ident[:].unsqueeze(1).to_broadcast([P, NT, P]), ALU.add).then_inc(xt_ok, 1)
                dve.wait_ge(qk_ps, d + 1)
                TT(qkT, PS[4][:], dT, ALU.mult).then_inc(qkt_ok, 1)
                for l in range(1, LEVELS):
                    dve.wait_ge(lv_ps, d * 6 + l)
                    if l < LEVELS - 1:
                        TT(Xi, Xi, PS[5][:], ALU.add)
                    TT(XiT, XiT, PS[6][:], ALU.add).then_inc(lv_ok, 1)
                    if l in (3, 5) and s is not None:
                        conv(s, l // 4)
                for n in range(NT - 1):
                    dve.wait_ge(s_ps, d * 3 + (n + 1))
                    if n == 0:
                        cpv(S, PS[6][:, 0:P]).then_inc(s_ok, 1)
                    else:
                        dve.wait_ge(s_ok, d * 3 + n)
                        STT(out=S, in0=S, scalar=egl[:, ds(d * NT + n, 1)], in1=PS[6][:, 0:P],
                            op0=ALU.mult, op1=ALU.add).then_inc(s_ok, 1)
                if s is not None:
                    conv(s, 2)
                dve.wait_ge(ro_ok, d + 1)
                link(STT(out=t1, in0=PS[7][:], scalar=cols[:, 104:105], in1=rB, op0=ALU.mult, op1=ALU.mult))
                TT(OT[:, ds(d, 1), :].rearrange("p a t -> p (a t)"), t1, gate_s, ALU.mult).then_inc(ot_ok, 1)

            for m in range(3):
                conv(0, m)
            delta(0, 1)
            with dve.Fori(1, H - 1) as d:
                link.enter(d - 1, 2 + 3 * (CONV - 1))
                delta(d, d + 1)
                link.leave(H - 2)
            delta(H - 1, None)

            ymul = sq_junk

            def out_projection(layer):
                base = layer * (2 * NT + 1)
                dve.wait_ge(gate_in, 16 * (2 * layer + 1))
                for u in range(2 * NT):
                    nh, n = u // NT, u % NT
                    cs = slice(nh * 512, nh * 512 + 512)
                    dve.wait_ge(wo_ps, layer * 2 * NT + u + 1)
                    link(TT(ymul[:, 0:512], PS[u % 2][:], gateB[:, cs], ALU.mult))
                    TT(X[:, n, cs], X[:, n, cs], ymul[:, 0:512], ALU.add).then_inc(wo_ok, 1)
                    dve.wait_ge(wo_ok, base + u + 1)

            def route(i):
                red = nc.vector.tensor_reduce
                b4 = lambda ap, w: ap.unsqueeze(2).to_broadcast([P, NT, w])
                iot = lambda w: iota_e[:, 0:w].unsqueeze(1).to_broadcast([P, NT, w])
                dve.wait_ge(r_ps, i + 1)
                link(TT(lg, PS[4][:, 0:NT * (NG + NE)].rearrange("p (n c) -> p n c", n=NT),
                        routB[:, i, :].unsqueeze(1).to_broadcast([P, NT, NG + NE]), ALU.add))
                grp, exp_l = lg[:, :, 0:NG], lg[:, :, NG:]

                def first_max(src, w, mval, onehot, scratch):
                    link(red(mval, src, AX_X, ALU.max))
                    link(TT(scratch, src, b4(mval, w), ALU.is_equal))
                    link(STT(out=scratch, in0=scratch, scalar=-1000.0, in1=iot(w), op0=ALU.mult, op1=ALU.add))
                    link(red(mi, scratch, AX_X, ALU.min))
                    link(TT(onehot, scratch, b4(mi, w), ALU.is_equal))

                first_max(grp, NG, gm, geq, gidx)
                link(TT(gidx, grp, b4(gm, NG), ALU.subtract))
                g_of = geq.unsqueeze(3).to_broadcast([P, NT, NG, EPG])
                e4 = lambda ap: ap.rearrange("p n (g e) -> p n g e", g=NG)
                link(TT(e4(el), e4(exp_l), g_of, ALU.mult))
                link(TS(e4(tmp32), g_of, -NEG, NEG, ALU.mult, ALU.add))
                link(TT(el, el, tmp32, ALU.add))
                first_max(el, NE, m1, oh1, tmp32)
                link(STT(out=el, in0=oh1, scalar=4 * NEG, in1=el, op0=ALU.mult, op1=ALU.add))
                first_max(el, NE, m2, oh2, tmp32)
                TT(both, oh1, oh2, ALU.add).then_inc(r_both, 1)
                TT(e21, m2, m1, ALU.subtract).then_inc(r_m, 1)
                dve.wait_ge(r_e, i + 1)
                link(red(gz, gidx, AX_X, ALU.add))
                link(nc.vector.reciprocal(gp, gz))
                link(TS(w1, e21, 1.0, None, ALU.add))
                link(nc.vector.reciprocal(w1, w1))
                link(TT(w1, w1, gp, ALU.mult))
                link(TT(w2, w1, e21, ALU.mult))
                for k, oh in enumerate((oh1, oh2)):
                    link(TT(ohd[k], oh, b4(dest1[:, k, :], NE), ALU.mult))
                dve.wait_ge(r_rank, i + 1)
                for k, oh in enumerate((oh1, oh2)):
                    link(TT(tmp32, PS[5][:, 0:NT * NE].rearrange("p (n e) -> p n e", n=NT), oh, ALU.mult))
                    link(red(posf[:, k, :], tmp32, AX_X, ALU.add))
                for b in range(NT):
                    if b > 0:
                        dve.wait_ge(r_pos, NT * i + b)
                        link(TS(posb, posf, -float(b * P), None, ALU.add))
                    if b >= 2:
                        dve.wait_ge(slots_ps, NT * i + b - 1)
                    place = place1 if b % 2 == 0 else place2
                    for u in range(2 * NT):
                        ins = TS(place[:, u, :], iota_r[:], (posb if b else posf)[:, u // NT, u % NT:u % NT + 1], None, ALU.is_equal)
                    ins.then_inc(r_pos, 1)
                    if b == 0:
                        slot_table(i, 0, 1)
                slot_table(i, 1, NT)
                cnt = PS[5][:, NT * NE:(NT + 1) * NE]
                link(TS(over_n, cnt, P + 0.5, None, ALU.is_gt))
                for b in range(2, NT):
                    link(STT(out=over_n, in0=cnt, scalar=b * P + 0.5, in1=over_n, op0=ALU.is_gt, op1=ALU.add))
                row, col = iota_e[:].unsqueeze(2).to_broadcast([P, NE, NE]), iota_e[:].unsqueeze(1).to_broadcast([P, NE, NE])
                link(TT(lt, col, row, ALU.is_lt))
                link(TT(lt, lt, over_n.unsqueeze(1).to_broadcast([P, NE, NE]), ALU.mult))
                link(red(before_n, lt, AX_X, ALU.add))
                wide = lambda ap: ap.unsqueeze(1).to_broadcast([P, MORE, NE])
                link(TT(item_d, iota_e[:, 0:MORE].unsqueeze(2).to_broadcast([P, MORE, NE]), wide(before_n), ALU.subtract))
                link(TT(item_s, item_d, wide(over_n), ALU.is_lt))
                link(STT(out=item_s, in0=item_d, scalar=-0.5, in1=item_s, op0=ALU.is_gt, op1=ALU.mult))
                link(TT(item_v, item_s, wide(iota_e[:]), ALU.mult))
                link(red(item_f[:, 0, :], item_v, AX_X, ALU.add))
                link(TT(item_v, item_s, item_d, ALU.mult))
                link(red(item_f[:, 1, :], item_v, AX_X, ALU.add))
                link(TS(item_f[:, 2, :], item_f[:, 1, :], float(NE), float(NE), ALU.mult, ALU.add))
                link(TT(item_f[:, 1, :], item_f[:, 2, :], item_f[:, 0, :], ALU.add))
                link(red(mi[:, 0:1], over_n, AX_X, ALU.add))
                cpv(nextra, mi[:, 0:1])
                cpv(item_i, item_f[:, 0:2, :].rearrange("p a j -> p (a j)")).then_inc(idx_ok, 1)

            def slot_table(i, b0, b1):
                cs = slice(b0 * NE, b1 * NE)
                dve.wait_ge(slots_ps, NT * i + b1)
                link(TS(slot_t[:, cs], PS[4][:, cs], 0.5, float(NO_ROW), ALU.is_lt, ALU.mult))
                link(STT(out=slot_f[:, cs], in0=PS[4][:, cs], scalar=-1.0, in1=slot_t[:, cs], op0=ALU.add, op1=ALU.add))
                cpv(slot_i[:, cs], slot_f[:, cs])
                link(TS(slot_t[:, cs], slot_f[:, cs], T - 0.5, float(-T), ALU.is_ge, ALU.mult))
                ins = TT(slot_g[:, cs], slot_f[:, cs], slot_t[:, cs], ALU.add)
                if b0 == 0:
                    ins.then_inc(idx_ok, 1)
                else:
                    link(ins)

            def experts(i):
                m = M
                B = i * NE

                def rows(e, u):
                    dve.wait_ge(m["xt_ps"], e + (B + 1))
                    if not isinstance(e, int) or e >= 2:
                        dve.wait_ge(m["gu_ps"], e + (B - 1))
                    cpv(xgT[u][:, 4:8, :], PS[3][:].rearrange("p (k j) -> p k j", k=4)).then_inc(m["xt_b"], 1)

                def product(e, u):
                    dve.wait_ge(m["sg"], e + (B + 1))
                    if not isinstance(e, int) or e >= 2:
                        dve.wait_ge(m["at_ps"], e + (B - 1))
                    TT(ac[u], sg[u], PS[u][:, DE:2 * DE], ALU.mult).then_inc(m["ac"], 1)

                def result(e, u, y_n):
                    dve.wait_ge(m["dn_ps"], e + (B + 1))
                    if y_n is not None:
                        dve.wait_ge(m["y"][u], y_n + 8 * B)
                    cpv(yo[u][:, 512:D], PS[7][:]).then_inc(m["yb"], 1)

                def step(e, q, y_n, more=True):
                    product(e, q % 2)
                    if not isinstance(e, int) or e >= 1:
                        if more:
                            rows(e + 1, (q + 1) % 2)
                        result(e - 1, (q + 1) % 2, y_n)

                rows(0, 0)
                rows(1, 1)
                for e in range(0, 5):
                    step(e, e % 4, 16 * ((e - 1) // 2) if e > 2 else None)
                with dve.Fori(0, 6) as j:
                    for q in range(4):
                        e0 = 5 + q
                        step(j * 4 + e0, e0 % 4, (j * 2 + (e0 - 1) // 2) * 16)
                for e in range(29, NE):
                    step(e, e % 4, 16 * ((e - 1) // 2), more=(e < NE - 1))
                result(NE - 1, 1, 16 * (NE // 2 - 1))

                xm = MX[i]
                dve.wait_ge(idx_ok, 2 * i + 2)
                n_x = dve.value_load(nextra[0:1, 0:1], min_val=0, max_val=MORE)
                with dve.If(n_x > 0):
                    with dve.Fori(0, n_x) as j:
                        dve.wait_ge(xm["stage"], stage_n("xt_ps", j))
                        cpv(xgT[0][:, 0:4, :], PS[2][:].rearrange("p (k j) -> p k j", k=4))
                        cpv(xgT[0][:, 4:8, :], PS[3][:].rearrange("p (k j) -> p k j", k=4)).then_inc(xm["stage"], 1)
                        dve.wait_ge(xm["stage"], stage_n("sg", j))
                        TT(ac[0], sg[0], PS[0][:, DE:2 * DE], ALU.mult).then_inc(xm["stage"], 1)
                        dve.wait_ge(xm["stage"], stage_n("dn_ps", j))
                        cpv(yo[0][:, 0:512], PS[6][:])
                        cpv(yo[0][:, 512:D], PS[7][:]).then_inc(xm["stage"], 1)
                with dve.Else():
                    dve.nop()
                dve.nop()

            def combine(i):
                dve.wait_ge(gate_in, 16 * (2 * i + 2))
                for n in range(NT):
                    dve.wait_ge(y_in[n], 32 * (i + 1))
                    link(TS(Y[:, 0, n, :], Y[:, 0, n, :], w1[:, n:n + 1], None, ALU.mult))
                    link(STT(out=Y[:, 1, n, :], in0=Y[:, 1, n, :], scalar=w2[:, n:n + 1], in1=Y[:, 0, n, :], op0=ALU.mult, op1=ALU.add))
                    link(TT(Y[:, 1, n, :], Y[:, 1, n, :], gateB[:], ALU.mult))
                    ins = TT(X[:, n, :], X[:, n, :], Y[:, 1, n, :], ALU.add)
                    if n < NT - 1:
                        link(ins)
                ins.then_inc(wo_ok, 1)
                dve.wait_ge(wo_ok, (i + 1) * (2 * NT + 1))

            out_projection(0)
            norm(1)
            route(0)
            experts(0)
            combine(0)

            norm(2)
            dve.wait_ge(forget_ps, 1)
            link(TT(tf1.rearrange("p (n c) -> p n c", n=NT), PS[4][:, 0:NT * 2 * H].rearrange("p (n c) -> p n c", n=NT),
                    bfb[:].unsqueeze(1).to_broadcast([P, NT, 2 * H]), ALU.add))
            link(TS(tf2, tf1, -1.0, None, ALU.mult))
            TT(tf2, tf2, tf1, ALU.min).then_inc(forget_dve, 1)
            dve.wait_ge(forget_act, 1)
            STT(out=lf, in0=tf1, scalar=0.0, in1=tf2, op0=ALU.min, op1=ALU.subtract).then_inc(forget_dve, 1)
            dve.wait_ge(forget_ps, 2)
            TS(cumn.rearrange("p (c n) -> p n c", c=2 * H), PS[5][:, 0:NT * 2 * H].rearrange("p (n c) -> p n c", n=NT),
               -1.0, None, ALU.mult).then_inc(forget_dve, 1)

            def attend(p):
                dve.wait_ge(fev, p * 4 + 4)
                after(dve, on_ok, p)
                link(TS(eg, eg, 1.0, None, ALU.add))
                nc.vector.reciprocal(sgate, eg).then_inc(sgt_ok, 1)
                dve.wait_ge(fr_ok, p * 2 + 1)
                STT(out=qh, in0=qkr[0], scalar=cols[:, 105:106], in1=sqr[0], op0=ALU.mult, op1=ALU.mult).then_inc(qkh_ok, 1)
                dve.wait_ge(fr_ok, p * 2 + 2)
                STT(out=kh, in0=qkr[1], scalar=cols[:, 106:107], in1=sqr[1], op0=ALU.mult, op1=ALU.mult).then_inc(qkh_ok, 1)
                for u in range(8):
                    a, qt = u // NT, u % NT
                    w = (qt + 1) * P
                    dve.wait_ge(sc_ps, p * 8 + (u + 1))
                    if qt == 0:
                        dve.wait_ge(cbt_ok, p * 2 + (a + 1))
                    after(dve, pr_ok, p * 8 + (u - 1))
                    dve.sem_inc(dve_passed, 1)
                    link(nc.vector.tensor_tensor_reduce(out=sS[u % 2][:, 0:w], in0=PS[2 + u % 2][:, 0:w],
                                                        in1=cbT[a][:, offs[qt]:offs[qt] + w], scale=1.0, scalar=3 * NEG,
                                                        op0=ALU.add, op1=ALU.max, accum_out=mx[:, u:u + 1]))
                    if u == 0:
                        after(dve, pr_ok, p * 8)
                    TS(nmx[:, u:u + 1], mx[:, u:u + 1], -1.0, None, ALU.mult).then_inc(sc_ok, 1)
                dve.wait_ge(pr_ok, p * 8 + 8)
                link(nc.vector.reciprocal(rinv, rsum))
                dve.wait_ge(pv_ps, p * 8 + 8)
                after(dve, ont_ps, p)
                ri = rinv.rearrange("p (a n) -> p n a", a=2).unsqueeze(3).to_broadcast([P, NT, 2, 64])
                link(TT(on.rearrange("p n (a c) -> p n a c", a=2), PS[6][:].rearrange("p (n a c) -> p n a c", n=NT, a=2), ri, ALU.mult))
                TT(on, on, sgate, ALU.mult).then_inc(on_ok, 1)

            attend(0)
            with dve.Fori(1, H) as p:
                link.enter(p - 1, 11)
                attend(p)
                link.leave(H - 1)

            out_projection(1)
            norm(3)
            route(1)
            experts(1)
            combine(1)

            dve.wait_ge(n_rs, 5)
            dve.wait_ge(fin_w, 16)
            for n in range(NT):
                STT(out=X[:, n, :], in0=X[:, n, :], scalar=rstd[:, n:n + 1], in1=shiftB[:], op0=ALU.mult, op1=ALU.mult).then_inc(fin_ok, 1)

        @block.gpsimd
        def _(pool):
            g = nc.gpsimd
            link = Link(pool, pool_link, pool_passed)

            def passed():
                pool.sem_inc(pool_passed, 1)

            g.memset(rows_in[:], 0.0)
            g.memset(bias_row[:], 0.0).then_inc(consts, 1)
            g.memset(ones[:], 1.0)
            link(g.memset(ident[:], 0.0))
            sel = g.affine_select
            sel(out=ident[:], in_=ident[:], pattern=[[-1, P]], compare_op=ALU.not_equal, fill=1.0, base=0, channel_multiplier=1)
            sel(out=upto[:], in_=ones[:], pattern=[[1, P]], compare_op=ALU.is_ge, fill=0.0, base=0, channel_multiplier=-1).then_inc(consts, 1)
            sel(out=before[:], in_=ones[:], pattern=[[1, P]], compare_op=ALU.is_ge, fill=0.0, base=-1, channel_multiplier=-1)
            link(g.memset(halves[:], 0.0))
            g.memset(halves[0:64, 0:64], 1.0)
            g.memset(halves[64:P, 64:P], 1.0).then_inc(consts, 1)
            pool.wait_ge(consts, 3)
            g.memset(eps_c[:, 0:1], EPS)
            g.memset(eps_c[:, 1:2], 1.0)
            g.memset(eps_c[:, 2:3], float(np.log(P ** -0.5)))
            g.memset(eps_c[:, 3:4], float(np.log(64 ** -0.5)))
            g.iota(hT[:, 0, 0:P].bitcast(I32), pattern=[[1, P]], base=0, channel_multiplier=0)
            g.iota(hT[:, 0, P:2 * P].bitcast(I32), pattern=[[0, P]], base=0, channel_multiplier=1)
            g.iota(hT[:, 3, 0:2 * NT].bitcast(I32), pattern=[[T, 2], [P, NT]], base=1, channel_multiplier=1)
            link(g.iota(iota_i[:], pattern=[[1, NE]], base=0, channel_multiplier=0))
            g.tensor_copy(iota_e[:], iota_i[:])
            g.tensor_copy(iota_r[:], hT[:, 0, 0:P].bitcast(I32))
            g.tensor_copy(dest1[:].rearrange("p k n -> p (k n)"), hT[:, 3, 0:2 * NT].bitcast(I32)).then_inc(consts, 1)
            pool.wait_ge(consts, 4)

            pool.wait_ge(decay_dve, 4)
            for u in range(2):
                g.memset(cin[u][:, 0:CONV - 1], 0.0)

            def head_rows(s):
                after(pool, conv_ok, s * 3)
                if not isinstance(s, int):
                    passed()
                g.tensor_copy(taps[:].unsqueeze(2), cols[:, 0:3 * CONV * KD].rearrange("p (c h) -> p c h", h=KD)[:, :, ds(s, 1)])
                g.tensor_copy(lah[:, 0, :], la[:, ds(s * NT, NT)])
                g.tensor_copy(lah[:, 1, :], beta[:, ds(s * NT, NT)]).then_inc(row_ok, 1)

            def ada_item(d, q, par):
                slot = (par + q) % 2
                if isinstance(d, int):
                    n_in = 32 * ((ADA_FIRST + 5 * d + q) // 2 + 1)
                else:
                    n_in = (d * 5 + (ADA_FIRST + q + 2 - slot)) * 16
                pool.wait_ge(ada_in[slot], n_in)
                passed()
                pool.wait_ge(ada_ps, d * 5 + (ADA_FIRST + q - 1))
                passed()
                w = Dr[:, slot, :].rearrange("p (k n) -> p k n", k=KD)
                link(g.tensor_tensor(w, w, cact[:].unsqueeze(2).to_broadcast([P, KD, ADA_W]), ALU.mult))
                for half in (4, 2, 1):
                    link(g.tensor_tensor(w[:, 0:half], w[:, 0:half], w[:, half:2 * half], ALU.add))
                ins = g.tensor_tensor(ada_acc[:, slot, :], w[:, 0, :], bias_row[:, slot, :], ALU.add)
                ins.then_inc(ada_sum2, 1)

            def delta(d, s, par):
                pool.wait_ge(diff_ok, d + 1)
                passed()
                g.affine_select(out=t4(dT), in_=t4(dT), pattern=[[0, NT], [1, P]], compare_op=ALU.is_ge, fill=NEG,
                                base=0, channel_multiplier=-1).then_inc(msk_ok, 1)
                ada_item(d, 0, par)
                pool.wait_ge(at_ok, d + 1)
                for l in range(1, LEVELS):
                    if l == LEVELS - 1:
                        pool.wait_ge(qk_ps, d + 1)
                        passed()
                    g.tensor_tensor(t4(nt[l]), t4(aT), negmask[:, l:l + 1, :].to_broadcast([P, NT, P]), ALU.mult).then_inc(nt_ok, 1)
                if s is not None:
                    head_rows(s)
                ada_item(d, 1, par)
                ada_item(d, 2, par)
                ada_item(d, 3, par)
                ada_item(d, 4, par)

            pool.wait_ge(cols_ok, 1)
            pool.wait_ge(act_setup, 2)
            head_rows(0)
            delta(0, 1, 0)
            with pool.Fori(0, 3) as j:
                link.enter(j, 2 * ADA_PER_HEAD * 4)
                delta(j * 2 + 1, j * 2 + 2, 1)
                delta(j * 2 + 2, j * 2 + 3, 0)
                link.leave(3)
            delta(7, None, 1)

            def experts(i):
                m = M
                B = i * NE
                rows_of = h_rows[i]
                pool.sem_inc(MX[i]["next"], 1)
                pool.wait_ge(wo_ps, (i + 1) * 2 * NT)
                for u in range(4):
                    ins = g.memset(xg[u], 0.0)
                link(ins)
                pool.wait_ge(idx_ok, 2 * i + 1)
                for u in range(2):
                    pool.wait_ge(hr_out[u], 16 * 2 * (i + 1))

                def gather(e, u):
                    g.indirect_dma_start(out=xg[u], out_offset=None, in_=rows_of,
                                         in_offset=bass.IndirectOffsetOnAxis(ap=gidx_i[:, u, :], axis=0),
                                         bounds_check=T - 1, oob_is_err=False).then_inc(m["xg"][u], 16)

                def pick(e, u):
                    g.tensor_copy(gidx_i[:, u, :], slot_g[:, ds(e, 1)]).then_inc(m["cp"], 1)

                def scatter(e, u):
                    g.indirect_dma_start(out=y_rows[i], out_offset=bass.IndirectOffsetOnAxis(ap=sidx[:, u, :], axis=0),
                                         in_=yo[u], in_offset=None, bounds_check=2 * T - 1,
                                         oob_is_err=False).then_inc(m["y"][u], 16)

                for e in range(4):
                    pick(e, e)
                    pool.wait_ge(m["cp"], 2 * B + e + 1)
                    gather(e, e)

                def step(e, q, cp_n, y_n, more=True):
                    u = q % 2
                    if more:
                        pool.wait_ge(m["xt_ps"], e + (B + 1))
                        passed()
                        pick(e + 4, q)
                        pool.wait_ge(m["cp"], cp_n + (2 * B + 1))
                        passed()
                        gather(e + 4, q)
                        cp_n = cp_n + 1
                    if y_n is not None:
                        pool.wait_ge(m["y"][u], y_n + 8 * B)
                        passed()
                    g.tensor_copy(sidx[:, u, :], slot_i[:, ds(e, 1)]).then_inc(m["cp"], 1)
                    pool.wait_ge(m["cp"], cp_n + (2 * B + 1))
                    pool.wait_ge(m["ya"], e + (B + 1))
                    pool.wait_ge(m["yb"], e + (B + 1))
                    passed()
                    scatter(e, u)

                for e in range(4):
                    step(e, e, 4 + 2 * e, 16 * (e // 2) if e >= 2 else None)
                with pool.Fori(1, NE // 4 - 1) as j:
                    for q in range(4):
                        step(j * 4 + q, q, j * 8 + (4 + 2 * q), (j * 2 + q // 2) * 16)
                for q in range(4):
                    step(NE - 4 + q, q, 2 * NE - 4 + q, 16 * (NE // 2 - 2 + q // 2), more=False)
                for u in range(2):
                    pool.wait_ge(m["y"][u], 8 * B + 16 * (NE // 2))

                xm = MX[i]
                pool.wait_ge(idx_ok, 2 * i + 2)
                n_x = pool.value_load(nextra[0:1, 0:1], min_val=0, max_val=MORE)
                with pool.If(n_x > 0):
                    with pool.Fori(0, n_x) as j:
                        c = pool.value_load(item_i[0:1, ds(j + MORE, 1)], min_val=NE, max_val=NT * NE - 1)
                        g.tensor_copy(gidx_i[:, 0, :], slot_g[:, ds(c, 1)])
                        g.tensor_copy(sidx[:, 0, :], slot_i[:, ds(c, 1)]).then_inc(xm["stage"], 1)
                        pool.wait_ge(xm["stage"], stage_n("idx", j))
                        passed()
                        g.indirect_dma_start(out=xg[0], out_offset=None, in_=rows_of,
                                             in_offset=bass.IndirectOffsetOnAxis(ap=gidx_i[:, 0, :], axis=0),
                                             bounds_check=T - 1, oob_is_err=False).then_inc(xm["moved"], 16)
                        pool.wait_ge(xm["stage"], stage_n("y", j))
                        passed()
                        g.indirect_dma_start(out=y_rows[i], out_offset=bass.IndirectOffsetOnAxis(ap=sidx[:, 0, :], axis=0),
                                             in_=yo[0], in_offset=None, bounds_check=2 * T - 1,
                                             oob_is_err=False).then_inc(xm["moved"], 16)
                        pool.wait_ge(xm["moved"], j * 32 + 32)
                        pool.sem_inc(xm["next"], 1)
                with pool.Else():
                    pool.nop()
                pool.sem_inc(m["done"], 1)

            experts(0)

            pool.wait_ge(forget_dve, 3)

            def attend(p):
                pool.wait_ge(fev, p * 4 + 4)
                after(pool, pv_ps, p * 8)
                passed()
                g.tensor_copy(vS, vraw).then_inc(vs_ok, 1)
                after(pool, cb_ps, p * 2)
                g.tensor_copy(nch.rearrange("p a n -> p (a n)"), cumn[:, ds(p * 2 * NT, 2 * NT)]).then_inc(nch_ok, 1)
                for a in range(2):
                    pool.wait_ge(cb_ok, p * 2 + (a + 1))
                    if a == 0:
                        after(pool, sc_ok, p * 8)
                    passed()
                    for qt in range(NT):
                        w = (qt + 1) * P
                        last = g.affine_select(out=cbT[a][:, offs[qt]:offs[qt] + w], in_=cbS[:, a, 0:w], pattern=[[-1, w]],
                                               compare_op=ALU.is_ge, fill=NEG, base=qt * P, channel_multiplier=1)
                    last.then_inc(cbt_ok, 1)

            attend(0)
            with pool.Fori(1, H) as p:
                attend(p)
            experts(1)


_INS = ['x', 'c', 'ada_w', 'ada_b', 'gdn_w_in', 'gdn_conv', 'gdn_a_log', 'gdn_dt_bias', 'gdn_norm', 'gdn_w_out',
        'fox_w_in', 'fox_b_f', 'fox_q_norm', 'fox_k_norm', 'fox_w_out', 'moe_w_group', 'moe_b_group',
        'moe_w_router', 'moe_b_router', 'moe_w_gate_up', 'moe_w_down', 'final_norm']


def kernel(**inputs):
    import numpy as _np
    import concourse.bacc as _bacc
    from concourse import mybir as _mybir
    from concourse.bass_utils import run_bass_kernel_spmd as _run

    nc = _bacc.Bacc("TRN2", target_bir_lowering=False, num_devices=1)
    arrays, args = {}, []
    for name in _INS:
        a = _np.ascontiguousarray(inputs[name])
        arrays[f"in_{name}_dram"] = a
        args.append(nc.dram_tensor(f"in_{name}_dram", a.shape, _mybir.dt.from_np(a.dtype), kind="ExternalInput").ap())
    args.append(nc.dram_tensor("out_0_dram", (1, T, D), F32, kind="ExternalOutput").ap())
    build(nc, *args)
    r = _run(nc, [arrays], core_ids=[0])
    return r.results[0]["out_0_dram"]
```

```python
from contextlib import ExitStack

import numpy as np

import concourse.bass as bass
from concourse import mybir

F32 = mybir.dt.float32
F32R = mybir.dt.float32r
I32 = mybir.dt.int32
ALU = mybir.AluOpType
ACT = mybir.ActivationFunctionType
AX_X = mybir.AxisListType.X

P = 128
T, D = 512, 1024
NT, KD = T // P, D // P
H = 8
NG, EPG = 4, 8
NE = NG * EPG
DE = 256
CONV = 4
LEVELS = 7
EPS = 1e-6
ADA_W = 256
ADA_FIRST = 8
ADA_PER_HEAD = 5
ADA_LEVELS = (2, 4, 6)
PIECES = ((), (0, 1), (2,), (3,), (4, 5), (6,), (7,))
NEG = -1e30
WO = 3 * NT
MIX_W = 64 * H // 2 + 16
MORE = 7
NO_ROW = 8192
GDN, FOX = 0, 1


def ds(i, n):
    return bass.ds(i, n)


class Link:

    def __init__(self, eng, sem, passed=None):
        self.eng, self.sem, self.base, self.k, self.passed = eng, sem, 0, 0, passed

    def __call__(self, ins):
        self.k += 1
        ins.then_inc(self.sem, 1)
        self.eng.wait_ge(self.sem, self.base + self.k)
        if self.passed is not None and not isinstance(self.base, int):
            self.eng.sem_inc(self.passed, 1)

    def enter(self, i, per):
        self.start, self.per = self.base + self.k, per
        self.base, self.k = i * per + self.start, 0

    def leave(self, n):
        assert self.k == self.per, f"links per iteration: {self.k}"
        self.base, self.k = self.start + n * self.per, 0


def after(eng, sem, n):
    if not isinstance(n, int) or n > 0:
        eng.wait_ge(sem, n)


def build(nc, x, c, ada_w, ada_b, gdn_w_in, gdn_conv, gdn_a_log, gdn_dt_bias, gdn_norm, gdn_w_out,
          fox_w_in, fox_b_f, fox_q_norm, fox_k_norm, fox_w_out, moe_w_group, moe_b_group,
          moe_w_router, moe_b_router, moe_w_gate_up, moe_w_down, final_norm, out):
    ctx = ExitStack()
    with ctx:
        def sb(name, shape, dt=F32):
            return ctx.enter_context(nc.sbuf_tensor(name, shape, dt))

        def sb_over(tensor_at, name, shape):
            return nc.alloc_sbuf_tensor_at(name, shape, F32R, offset=tensor_at)

        def sb_next():
            return -(-nc.sbuf_base // 32) * 32

        def sem(name):
            return ctx.enter_context(nc.semaphore(name))

        def sems(name, n):
            return [sem(f"{name}{i}") for i in range(n)]

        ada_rows = nc.dram_tensor("ada_rows", (2, 6 * D), F32, kind="Internal").ap()
        h_rows = [nc.dram_tensor(f"h_rows{i}", (T, D), F32, kind="Internal").ap() for i in range(2)]
        x_rows = nc.dram_tensor("x_rows", (T, D), F32, kind="Internal").ap()
        y_rows = [nc.dram_tensor(f"y_rows{i}", (2 * T, D), F32, kind="Internal").ap() for i in range(2)]

        x_at = sb_next()
        X = sb("X", [P, NT, D])
        hT_at = sb_next()
        hT = sb("hT", [P, KD, T])
        wr_at = sb_next()
        Wr = sb("Wr", [P, 4, KD, 512])
        hHi = sb_over(x_at, "hHi", [P, KD, T])
        hLo = sb_over(hT_at, "hLo", [P, KD, T])
        Wlo = sb_over(wr_at, "Wlo", [P, 2 * KD, 512])
        Whi = sb_over(wr_at + 2 * KD * 512 * 4, "Whi", [P, 2 * KD, 512])
        Dr = sb("Dr", [P, 2, 2048])
        shiftB = sb("shiftB", [P, D])
        scaleB = sb("scaleB", [P, D])
        gateB = sb("gateB", [P, D])
        ident = sb("ident", [P, P])
        ones = sb("ones", [P, P])
        upto = sb("upto", [P, P])
        before = sb("before", [P, P])
        halves = sb("halves", [P, P])
        negmask = sb("negmask", [P, LEVELS, P])
        rows_in = sb("rows_in", [P, P])
        cols = sb("cols", [P, P])
        cact = sb("cact", [P, KD])
        nega = sb("nega", [P, H])
        dtb = sb("dtb", [P, H])
        bfb = sb("bfb", [P, 2 * H])
        routB = sb("routB", [P, 2, NG + NE])
        routW = sb("routW", [P, 2, KD, NG + NE])
        abW = sb("abW", [P, KD, 2 * H])
        fW = sb("fW", [P, KD, 2 * H])
        taps = sb("taps", [P, 3 * CONV])
        iota_i = sb("iota_i", [P, NE], I32)
        iota_e = sb("iota_e", [P, NE])
        iota_r = sb("iota_r", [P, P])
        dest1 = sb("dest1", [P, 2, NT])
        bias_row = sb("bias_row", [P, 2, ADA_W])
        ada_acc = sb("ada_acc", [P, 2, ADA_W])
        ada_row = sb("ada_row", [1, 2, ADA_W])
        ss = sb("ss", [P, NT])
        rstd = sb("rstd", [P, NT])
        eps_c = sb("eps_c", [P, 4])
        AR = 33 * 512
        arena = sb("arena", [P, AR])

        class Carve:

            def __init__(self, at=0):
                self.at = at

            def __call__(self, *shape, dt=None):
                n = int(np.prod(shape))
                v = arena[:, self.at:self.at + n]
                self.at += n
                assert self.at <= AR, self.at
                if dt is not None:
                    v = v.bitcast(dt)
                if len(shape) == 2:
                    v = v.rearrange("p (a b) -> p a b", a=shape[0])
                if len(shape) == 3:
                    v = v.rearrange("p (a b c) -> p a b c", a=shape[0], b=shape[1])
                return v

        cv = Carve()
        OT = cv(KD, T)
        after_ot = cv.at
        cv = Carve(after_ot)
        hrow = [cv(D) for _ in range(2)]
        sq_junk = cv(D)
        ymul = cv(512)
        bias_first = arena[0:1, 8 * D:10 * D]

        def first_item(a):
            flat = Wr[:, 1:4].rearrange("p s k n -> p (s k n)")
            v = flat[:, a * 2048:(a + 1) * 2048] if a < 6 else Dr[:, a - 6, :]
            return v.rearrange("p (k n) -> p k n", k=KD)

        cv = Carve(after_ot)
        cin = [cv(T + CONV - 1) for _ in range(2)]
        cv.at += 2
        qkv = [cv(T) for _ in range(3)]
        gate_s = cv(T)
        sqk, sqq = cv(T), cv(T)
        egB, dT = cv(T), cv(T)
        khat, qhat, kb, qg = cv(T), cv(T), cv(T), cv(T)
        vb, kwn, kdec_k = cv(T), cv(T), cv(T)
        XiT = cv(T)
        aT, qkT, Xi = sqk, sqq, egB
        nt = [XiT] + [cv(T) for _ in range(LEVELS - 2)] + [khat]
        vnew = cv(2, P)
        S = cv(P)
        la, gc, beta, nbeg, kdecay, egl, t_ab, t_ab2 = (cv(H * NT) for _ in range(8))
        lah = cv(2, NT)
        Pp, nWT, osq, rB, t1 = kb, qhat, egB, dT, khat
        cv = Carve(after_ot)
        qkr = [cv(T) for _ in range(2)]
        sqr = [cv(T) for _ in range(2)]
        vraw, eg, vS, sgate, on = cv(NT, P), cv(NT, P), cv(NT, P), cv(NT, P), cv(NT, P)
        qh, kh = cv(T), cv(T)
        cbS = cv(2, T)
        offs = [0, 128, 384, 768]
        cbT = [cv(1280) for _ in range(2)]
        sS = [cv(T) for _ in range(2)]
        pS = [cv(T) for _ in range(2)]
        pT = [cv(T) for _ in range(2)]
        cumn = cv(NT * 2 * H)
        lf, tf1, tf2 = pS[0][:, 0:NT * 2 * H], sS[0][:, 0:NT * 2 * H], sS[1][:, 0:NT * 2 * H]
        nch = cv(2, NT)
        mx, nmx, rsum = cv(8), cv(8), cv(8)
        rinv = cv(8)
        cv = Carve()
        xg = [cv(D) for _ in range(4)]
        xgT = [cv(KD, P) for _ in range(2)]
        sg = [cv(DE) for _ in range(2)]
        ac = [cv(DE) for _ in range(2)]
        acT = [cv(2, P) for _ in range(2)]
        yo = [cv(D) for _ in range(2)]
        assert cv.at <= 12288
        place1 = cv(2 * NT, P)
        lt = cv(NE, NE)
        cv.at = 12288
        lg = cv(NT, NG + NE)
        gm, gz, gp, m1, m2, e21, w1, w2 = (cv(NT) for _ in range(8))
        geq, gidx = cv(NT, NG), cv(NT, NG)
        el, oh1, oh2, tmp32 = (cv(NT, NE) for _ in range(4))
        both = cv((NT + 1) * NE)
        ohd = [cv(NT, NE) for _ in range(2)]
        mi = cv(NT)
        posf = cv(2, NT)
        posb = cv(2, NT)
        slot_f = cv(NT * NE)
        slot_t = cv(NT * NE)
        slot_i = cv(NT * NE, dt=I32)
        slot_g = cv(NT * NE, dt=I32)
        over_n, before_n = cv(NE), cv(NE)
        item_d, item_s, item_v = cv(MORE, NE), cv(MORE, NE), cv(MORE, NE)
        item_f = cv(3, MORE)
        item_i = cv(2 * MORE, dt=I32)
        nextra = cv(1, dt=I32)
        sidx = cv(3, 1, dt=I32)
        gidx_i = cv(4, 1, dt=I32)
        place2 = cv(2 * NT, P)
        Y = [arena[:, a:a + NT * D].rearrange("p (n d) -> p n d", n=NT) for a in (0, 8 * D)]

        PS = [ctx.enter_context(nc.psum_tensor(f"PS{i}", [P, 512], F32)) for i in range(8)]

        consts = sem("consts")
        small_in, small2_in = sem("small_in"), sem("small2_in")
        x_in = sem("x_in")
        cols_ps, cols_ok = sem("cols_ps"), sem("cols_ok")
        act_setup = sem("act_setup")
        dve_link, act_link, pool_link = sem("dve_link"), sem("act_link"), sem("pool_link")
        pool_passed, dve_passed = sem("pool_passed"), sem("dve_passed")
        ada_in = sems("ada_in", 2)
        ada_first = sems("ada_first", ADA_FIRST // 2)
        ada_pool, ada_dve = sem("ada_pool"), sem("ada_dve")
        ada_ps, ada_rowok = sem("ada_ps"), sem("ada_rowok")
        ada_out = sems("ada_out", 2)
        bc_in = sem("bc_in")
        gate_in = sem("gate_in")
        mix_w = sems("mix_w", 2)
        moe_w = sems("moe_w", 4)
        moe_d = sems("moe_d", 2)
        n_rs, n_h, n_tr, n_ta, n_tb = sem("n_rs"), sem("n_h"), sem("n_tr"), sem("n_ta"), sem("n_tb")
        h_hi, h_lo = sem("h_hi"), sem("h_lo")
        w_hi, w_lo, w_lo_pool = sem("w_hi"), sem("w_lo"), sem("w_lo_pool")
        x_out, x_back = sem("x_out"), sem("x_back")
        proj_ps = sem("proj_ps")
        ev_pj = sem("ev_pj")
        conv_ok = sem("conv_ok")
        sq_ok = sem("sq_ok")
        decay_ps, decay_act, decay_dve = sem("decay_ps"), sem("decay_act"), sem("decay_dve")
        row_ok, gb_ps, ss_ps = sem("row_ok"), sem("gb_ps"), sem("ss_ps")
        rr_ok = sem("rr_ok")
        diff_ok, msk_ok, dT_ok, egb_ok = sem("diff_ok"), sem("msk_ok"), sem("dT_ok"), sem("egb_ok")
        hat_ok, kb_ok, qg_ok = sem("hat_ok"), sem("kb_ok"), sem("qg_ok")
        v_ps, k_ps, kk_ps, qk_ps = sem("v_ps"), sem("k_ps"), sem("kk_ps"), sem("qk_ps")
        vb_ok, kd_ok, at_ok, qkt_ok, xt_ok = sem("vb_ok"), sem("kd_ok"), sem("at_ok"), sem("qkt_ok"), sem("xt_ok")
        nt_ok, x1_ps, x1_ok, p_ps, p_ok, lv_ps, lv_ok = (sem(n) for n in ("nt_ok", "x1_ps", "x1_ok", "p_ps", "p_ok", "lv_ps", "lv_ok"))
        wt_ps, wt_ok, vn_ps, vn_ok, s_ps, s_ok = (sem(n) for n in ("wt_ps", "wt_ok", "vn_ps", "vn_ok", "s_ps", "s_ok"))
        o_ps, osq_ok, sso_ps, ro_ok, ot_ok = (sem(n) for n in ("o_ps", "osq_ok", "sso_ps", "ro_ok", "ot_ok"))
        wo_ps, wo_ok, y1_ok = sem("wo_ps"), sem("wo_ok"), sem("y1_ok")
        fpj_ps, fev = sem("fpj_ps"), sem("fev")
        fs_ps, fr_ok, qkh_ok = sem("fs_ps"), sem("fr_ok"), sem("qkh_ok")
        nch_ok, vs_ok, sgt_ok = sem("nch_ok"), sem("vs_ok"), sem("sgt_ok")
        cb_ps, cb_ok, cbt_ok = sem("cb_ps"), sem("cb_ok"), sem("cbt_ok")
        sc_ps, sc_ok, pr_ok, pt_ps, pt_ok, pv_ps = (sem(n) for n in ("sc_ps", "sc_ok", "pr_ok", "pt_ps", "pt_ok", "pv_ps"))
        on_ok, ont_ps, ont_ok = sem("on_ok"), sem("ont_ps"), sem("ont_ok")
        r_ps, r_e, r_both, r_rank, r_pos, idx_ok = (sem(n) for n in ("r_ps", "r_e", "r_both", "r_rank", "r_pos", "idx_ok"))
        hr_out, y_in = sems("hr_out", 2), sems("y_in", NT)
        slots_ps = sem("slots_ps")
        fin_ok, fin_out = sem("fin_ok"), sem("fin_out")
        STAGES = ("idx", "xt_ps", "xt", "gu_ps", "sg", "ac", "at_ps", "at", "dn_ps", "y")
        stage_n = lambda name, j: j * len(STAGES) + (STAGES.index(name) + 1)
        M = {n: sem(f"moe_{n}") for n in ("xt_ps", "xt_a", "xt_b", "gu_ps", "sg", "ac", "at_ps", "at", "dn_ps", "ya", "yb", "cp")}
        M["xg"] = sems("moe_xg", 4)
        M["y"] = sems("moe_y", 2)
        M["done"] = sem("moe_done")
        MX = [{n: sem(f"more{i}_{n}") for n in ("gu_w", "dn_w", "moved", "stage")} for i in range(2)]

        block = ctx.enter_context(nc.Block())
        t4 = lambda ap: ap.rearrange("p (n j) -> p n j", n=NT)
        over = lambda ap: ap.unsqueeze(2).to_broadcast([P, NT, P])

        ada_v = ada_w.rearrange("l (k p) n -> l p k n", p=P)

        @block.sync
        def _(sp):
            def load(dst, src, s):
                sp.dma_start(dst, src).then_inc(s, 16)

            def ada_load(a, layer, col, free_sem, free_n):
                slot = a % 2
                after(sp, free_sem, free_n)
                load(Dr[:, slot, :].rearrange("p (k n) -> p k n", k=KD), ada_v[layer, :, :, ds(col, ADA_W)], ada_in[slot])
                load(bias_row[0:1, slot, :], ada_b[layer:layer + 1, ds(col, ADA_W)], ada_in[slot])

            def section_loads(w, h, slot, s):
                for m in range(4):
                    load(Wr[:, slot, :, m * P:m * P + P],
                         w[0, :, m * D:(m + 1) * D].rearrange("(k p) n -> p k n", p=P)[:, :, ds(h * P, P)], s)

            sp.wait_ge(consts, 1)
            load(rows_in[0:CONV * 24, :], gdn_conv.rearrange("a j (m p) -> (a j m) p", p=P), small_in)
            load(rows_in[96:104, :], c.rearrange("a (k p) -> (a k) p", p=P), small_in)
            load(rows_in[104:105, :], gdn_norm, small_in)
            for half in range(2):
                load(rows_in[105:106, 64 * half:64 * half + 64], fox_q_norm, small_in)
                load(rows_in[106:107, 64 * half:64 * half + 64], fox_k_norm, small_in)
            load(nega[:], gdn_a_log[0].partition_broadcast(P), small_in)
            load(dtb[:], gdn_dt_bias[0].partition_broadcast(P), small_in)
            load(bfb[:], fox_b_f[0].partition_broadcast(P), small_in)
            load(bias_first, ada_b[0:1, 0:2 * D], small_in)
            for a in range(ADA_FIRST):
                load(first_item(a), ada_v[0, :, :, a * ADA_W:(a + 1) * ADA_W], ada_first[a // 2])
                if a == 3:
                    load(X[:], x.rearrange("a (n p) d -> p (a n) d", p=P), x_in)
            section_loads(gdn_w_in, 0, 0, mix_w[0])
            load(abW[:], gdn_w_in[0, :, 4 * D:].rearrange("(k p) n -> p k n", p=P), small2_in)
            load(fW[:], fox_w_in[0, :, 4 * D:].rearrange("(k p) n -> p k n", p=P), small2_in)
            for i in range(2):
                load(routB[:, i, 0:NG], moe_b_group[i].partition_broadcast(P), small2_in)
                load(routB[:, i, NG:], moe_b_router[i].partition_broadcast(P), small2_in)
                load(routW[:, i, :, 0:NG], moe_w_group[i].rearrange("(k p) n -> p k n", p=P), small2_in)
                load(routW[:, i, :, NG:], moe_w_router[i].rearrange("(k p) n -> p k n", p=P), small2_in)
            sp.wait_ge(ada_ps, ADA_FIRST)
            section_loads(gdn_w_in, 1, 1, mix_w[1])

            def expert_load(i, e, slot):
                load(Wr[:, slot], moe_w_gate_up[i].rearrange("g e (k p) n -> (g e) p k n", p=P)[ds(e, 1)]
                     .rearrange("a p k n -> p (a k) n"), moe_w[slot])

            def down_load(i, e, slot):
                load(Dr[:, slot, :].rearrange("p (k n) -> p k n", k=2),
                     moe_w_down[i].rearrange("g e (k p) n -> (g e) p k n", p=P)[ds(e, 1)]
                     .rearrange("a p k n -> p (a k) n"), moe_d[slot])

            def ada_of_head(d, par, between):
                for q in range(ADA_PER_HEAD):
                    if q == 2:
                        between()
                    a = par + q
                    layer, col = (0, (d * 2 + 8 + q) * ADA_W) if q < 2 else (1, (d * 3 + (q - 2)) * ADA_W)
                    if isinstance(d, int) and d == 0 and q < 2:
                        ada_load(a, layer, col, ada_ps, ADA_FIRST)
                    elif q == 2:
                        ada_load(a, layer, col, ada_dve, d + 1)
                    else:
                        ada_load(a, layer, col, ada_pool, d * 4 + (q - 1 if q < 2 else q - 2))

            def head_load(h, slot):
                sp.wait_ge(proj_ps, (h - 1) * 4)
                section_loads(gdn_w_in, h, slot, mix_w[slot])

            def out_load(w, nh, slot, s):
                load(Wr[:, slot], w[0].rearrange("(k p) n -> p k n", p=P)[:, :, nh * 512:nh * 512 + 512], s)

            def after_projection(layer):
                sp.wait_ge((proj_ps, fpj_ps)[layer], 4 * H)
                out_load((gdn_w_out, fox_w_out)[layer], 1, 1, mix_w[1])
                if layer == 0:
                    load(X[:], x.rearrange("a (n p) d -> p (a n) d", p=P), x_back)
                else:
                    sp.wait_ge(x_out, 16 * NT)
                    load(X[:], x_rows.rearrange("(n p) d -> p n d", p=P), x_back)
                for e in range(2):
                    expert_load(layer, e, e + 2)

            def first_out_load():
                sp.wait_ge(proj_ps, 4 * 7)
                out_load(gdn_w_out, 0, 0, mix_w[0])

            ada_of_head(0, 0, lambda: head_load(2, 0))
            with sp.Fori(0, 2) as j:
                for u in range(2):
                    ada_of_head(j * 2 + (1 + u), (1 + u) % 2, lambda: head_load(j * 2 + (3 + u), (1 + u) % 2))
            ada_of_head(5, 1, lambda: head_load(7, 1))
            ada_of_head(6, 0, first_out_load)
            ada_of_head(7, 1, lambda: after_projection(0))

            def sublayer_rows(layer):
                for s in range(2):
                    if layer == 0:
                        sp.wait_ge(ada_out[s], 8 * ADA_PER_HEAD * H)
                if layer == 1:
                    sp.wait_ge(wo_ok, WO)
                load(gateB[:], ada_rows[layer, 2 * D:3 * D].partition_broadcast(P), gate_in)
                sp.wait_ge(n_h, 4 * 2 * layer + 4)
                load(shiftB[:], ada_rows[layer, 3 * D:4 * D].partition_broadcast(P), bc_in)
                load(scaleB[:], ada_rows[layer, 4 * D:5 * D].partition_broadcast(P), bc_in)

            def experts(i):
                m = M
                B = i * NE
                if i == 0:
                    sp.wait_ge(ada_pool, 4 * H)
                    sp.wait_ge(ada_dve, H)
                for e in range(2):
                    down_load(i, e, e)
                sp.wait_ge(wo_ps, i * 2 * NT + NT)
                expert_load(i, 2, 0)
                for n in range(NT):
                    sp.wait_ge(n_h, 4 * (2 * i + 1) + n + 1)
                    load(h_rows[i][n * P:n * P + P, :], hrow[n % 2], hr_out[n % 2])
                    if n == 1:
                        sp.wait_ge(wo_ps, (i + 1) * 2 * NT)
                        expert_load(i, 3, 1)
                sp.wait_ge(wo_ok, i * WO + 2 * NT)
                load(gateB[:], ada_rows[i, 5 * D:6 * D].partition_broadcast(P), gate_in)
                with sp.Fori(0, NE // 4 - 1) as j:
                    for u in range(4):
                        sp.wait_ge(m["gu_ps"], j * 4 + u + 1 + B)
                        expert_load(i, j * 4 + (u + 4), (u + 2) % 4)
                        sp.wait_ge(m["dn_ps"], j * 4 + u + 1 + B)
                        down_load(i, j * 4 + (u + 2), u % 2)
                sp.wait_ge(m["dn_ps"], B + NE - 3)
                down_load(i, NE - 2, 0)
                xm = MX[i]
                sp.wait_ge(idx_ok, 2 * i + 2)
                n_x = sp.value_load(nextra[0:1, 0:1], min_val=0, max_val=MORE)

                def item_load(dst, w, e, s):
                    load(dst, w[i].rearrange("g e (k p) n -> (g e) p k n", p=P)[ds(e, 1)]
                         .rearrange("a p k n -> p (a k) n"), s)

                down_slot = Dr[:, 0, :].rearrange("p (k n) -> p k n", k=2)
                sp.wait_ge(m["gu_ps"], B + NE - 3)
                with sp.If(n_x > 0):
                    e = sp.value_load(item_i[0:1, 0:1], min_val=0, max_val=NE - 1)
                    item_load(Wr[:, 2], moe_w_gate_up, e, xm["gu_w"])
                with sp.Else():
                    sp.nop()
                sp.wait_ge(m["dn_ps"], B + NE - 2)
                down_load(i, NE - 1, 1)
                sp.wait_ge(m["dn_ps"], B + NE - 1)
                with sp.If(n_x > 0):
                    e = sp.value_load(item_i[0:1, 0:1], min_val=0, max_val=NE - 1)
                    item_load(down_slot, moe_w_down, e, xm["dn_w"])
                with sp.Else():
                    sp.nop()
                with sp.If(n_x > 1):
                    with sp.Fori(1, n_x) as j:
                        e = sp.value_load(item_i[0:1, ds(j, 1)], min_val=0, max_val=NE - 1)
                        sp.wait_ge(xm["moved"], j * 32)
                        item_load(Wr[:, 2], moe_w_gate_up, e, xm["gu_w"])
                        item_load(down_slot, moe_w_down, e, xm["dn_w"])
                with sp.Else():
                    sp.nop()
                sp.nop()

            def combine_load(i):
                sp.wait_ge(M["done"], i + 1)
                for n in range(NT):
                    for k in range(2):
                        load(Y[k][:, n, :], y_rows[i][k * T + n * P:k * T + n * P + P, :], y_in[n])

            sublayer_rows(0)
            experts(0)
            def pair_load(p, slot, n):
                after(sp, fpj_ps, n * 4)
                section_loads(fox_w_in, p, slot, mix_w[slot])

            sp.wait_ge(n_h, 8)
            load(shiftB[:], ada_rows[1, 0:D].partition_broadcast(P), bc_in)
            load(scaleB[:], ada_rows[1, D:2 * D].partition_broadcast(P), bc_in)
            pair_load(0, 0, 0)
            combine_load(0)
            pair_load(1, 1, 0)
            for n in range(NT):
                sp.wait_ge(wo_ok, 2 * NT + n + 1)
                load(x_rows[n * P:n * P + P, :], X[:, n, :], x_out)
            with sp.Fori(0, 3) as j:
                for u in range(2):
                    pair_load(j * 2 + (2 + u), u, j * 2 + (1 + u))
            sp.wait_ge(fpj_ps, 4 * 7)
            out_load(fox_w_out, 0, 0, mix_w[0])
            after_projection(1)
            sublayer_rows(1)
            experts(1)
            sp.wait_ge(n_h, 16)
            load(shiftB[:], final_norm.partition_broadcast(P), bc_in)
            combine_load(1)
            for n in range(NT):
                sp.wait_ge(fin_ok, n + 1)
                load(out[0, n * P:n * P + P, :], X[:, n, :], fin_out)
            sp.wait_ge(fin_out, 16 * NT)

        @block.tensor
        def _(pe):
            mm = nc.tensor.matmul
            tr = nc.tensor.transpose

            def tile(ap, n):
                return ap[:, n * P:n * P + P]

            def norm_transposes(phase, n):
                pe.wait_ge(n_h, 4 * phase + n + 1)
                if n >= 2:
                    hT_ready(phase, n - 2)
                for k in range(KD):
                    last = tr(PS[2 + 2 * (n % 2) + k // 4][:, (k % 4) * P:(k % 4) * P + P],
                              hrow[n % 2][:, k * P:k * P + P], ident[:])
                last.then_inc(n_tr, 1)

            def hT_ready(phase, n):
                pe.wait_ge(n_ta, 4 * phase + n + 1)
                pe.wait_ge(n_tb, 4 * phase + n + 1)

            def narrow(phase, tiles, w, width):
                for n in tiles:
                    hT_ready(phase, n)
                    for k in range(KD):
                        last = mm(PS[6][:, n * width:(n + 1) * width], tile(hT[:, k, :], n), w[:, k, :],
                                  start=(k == 0), stop=(k == KD - 1))
                return last

            pe.wait_ge(consts, 3)
            pe.wait_ge(small_in, 16 * 11)
            tr(PS[0][:, 0:P], rows_in[:], ident[:]).then_inc(cols_ps, 1)
            pe.wait_ge(act_setup, 1)
            for a in range(ADA_FIRST):
                if a % 2 == 0:
                    pe.wait_ge(ada_first[a // 2], 32)
                if a >= 2:
                    pe.wait_ge(ada_rowok, a - 1)
                for k in range(KD):
                    mm(PS[2 + a % 2][:, 0:ADA_W], cact[:, k:k + 1].to_broadcast([P, P]), first_item(a)[:, k, :],
                       start=(k == 0), stop=False)
                mm(PS[2 + a % 2][:, 0:ADA_W], ones[0:1, :], bias_first[:, a * ADA_W:(a + 1) * ADA_W],
                   start=False, stop=True).then_inc(ada_ps, 1)
            for n in range(NT):
                norm_transposes(0, n)
                if n == 1:
                    pe.wait_ge(small2_in, 16 * 10)
                if n > 0:
                    narrow(0, [n - 1], abW, 2 * H)
            narrow(0, [NT - 1], abW, 2 * H).then_inc(decay_ps, 1)
            def mm3(out_ap, a_hi, a_lo, b_hi, b_lo, k):
                mm(out_ap, a_hi, b_hi, start=(k == 0), stop=False)
                mm(out_ap, a_hi, b_lo, start=False, stop=False)
                return mm(out_ap, a_lo, b_hi, start=False, stop=(k == KD - 1))

            def project(s, slot, a, b):
                for f in range(a, b):
                    m, k = f // KD, f % KD
                    if f == 0:
                        if isinstance(s, int) and s < 2:
                            pe.wait_ge(w_lo_pool, KD * (s + 1))
                        else:
                            pe.wait_ge(w_lo, (s - 1) * KD)
                    if m == 0 and isinstance(s, int) and s == 0:
                        pe.wait_ge(h_lo, k + 1)
                    if k == 0:
                        n = s * 4 + (m - 1)
                        after(pe, ev_pj, n)
                    last = mm3(PS[m % 2][:], Whi[:, slot * KD + k, m * P:m * P + P], Wlo[:, slot * KD + k, m * P:m * P + P],
                               hHi[:, k, :], hLo[:, k, :], k)
                    if k == KD - 1:
                        last.then_inc(proj_ps, 1)

            project(0, 0, 0, KD)
            pe.wait_ge(decay_dve, 2)
            mm(PS[5][:, 0:32], upto[:], la, start=True, stop=True)
            mm(PS[5][:, 32:64], ones[:], la, start=True, stop=True).then_inc(decay_ps, 1)

            def ada_item(d, q, par):
                if q == 0:
                    pe.wait_ge(ada_dve, d + 1)
                else:
                    pe.wait_ge(ada_pool, d * 4 + q)
                if q == 0:
                    pe.wait_ge(kd_ok, d + 1)
                else:
                    pe.wait_ge(ada_rowok, d * 5 + (ADA_FIRST + q))
                mm(PS[2][0:1, 0:ADA_W], ones[:, 0:1], ada_acc[:, (par + q) % 2, :], start=True, stop=True).then_inc(ada_ps, 1)

            def delta(d, fill, par):
                pe.wait_ge(row_ok, d + 1)
                after(pe, ada_rowok, d * 5 + ADA_FIRST)
                after(pe, ro_ok, d)
                for n in range(NT):
                    mm(tile(PS[2], n), lah[:, 0, n:n + 1].to_broadcast([P, P]), upto[:], start=True, stop=True)
                for n in range(NT):
                    last = mm(tile(PS[3], n), lah[:, 1, n:n + 1].to_broadcast([P, P]), ident[:], start=True, stop=True)
                last.then_inc(gb_ps, 1)
                fill(0, 7)
                pe.wait_ge(sq_ok, d + 1)
                mm(PS[4][:], ones[:], sqk, start=True, stop=True).then_inc(ss_ps, 1)
                mm(PS[5][:], ones[:], sqq, start=True, stop=True).then_inc(ss_ps, 1)
                after(pe, s_ok, d * 3)
                for n in range(NT):
                    last = tr(tile(PS[6], n), tile(qkv[2], n), ident[:])
                last.then_inc(v_ps, 1)
                fill(7, 9)
                pe.wait_ge(hat_ok, d + 1)
                pe.wait_ge(egb_ok, d + 1)
                for n in range(NT):
                    last = tr(tile(PS[2], n), tile(khat, n), ident[:])
                last.then_inc(k_ps, 1)
                fill(9, 10)
                pe.wait_ge(kb_ok, d + 1)
                for n in range(NT):
                    last = mm(tile(PS[3], n), tile(khat, n), tile(kb, n), start=True, stop=True)
                last.then_inc(kk_ps, 1)
                for n in range(NT):
                    last = mm(tile(PS[4], n), tile(khat, n), tile(qhat, n), start=True, stop=True)
                last.then_inc(qk_ps, 1)
                fill(10, 12)
                pe.wait_ge(xt_ok, d + 1)
                for n in range(NT):
                    last = tr(tile(PS[5], n), tile(XiT, n), ident[:])
                last.then_inc(x1_ps, 1)
                fill(12, 13)
                for l in range(1, LEVELS):
                    lv = d * (2 * LEVELS - 3) + 2 * l
                    if l == 1:
                        pe.wait_ge(x1_ok, d + 1)
                        pe.wait_ge(qkt_ok, d + 1)
                    else:
                        pe.wait_ge(lv_ok, lv - 3)
                    pe.wait_ge(nt_ok, d * 6 + l)
                    for n in range(NT):
                        last = mm(tile(PS[4], n), tile(nt[l], n), tile(Xi, n), start=True, stop=True)
                    last.then_inc(p_ps, 1)
                    fill(12 + l, 13 + l)
                    if l in ADA_LEVELS:
                        ada_item(d, ADA_LEVELS.index(l), par)
                    if l > 1:
                        pe.wait_ge(lv_ok, lv - 2)
                    pe.wait_ge(p_ok, d * 6 + l)
                    if l < LEVELS - 1:
                        for n in range(NT):
                            last = mm(tile(PS[5], n), tile(XiT, n), tile(Pp, n), start=True, stop=True)
                        last.then_inc(lv_ps, 1)
                    for n in range(NT):
                        last = mm(tile(PS[6], n), tile(Pp, n), tile(XiT, n), start=True, stop=True)
                    last.then_inc(lv_ps, 1)
                fill(19, 20)
                pe.wait_ge(lv_ok, (d + 1) * (2 * LEVELS - 3))
                for n in range(NT):
                    last = mm(tile(PS[4], n), tile(kwn, n), tile(XiT, n), start=True, stop=True)
                last.then_inc(wt_ps, 1)
                for n in range(NT):
                    last = mm(PS[5][:, 0:P], tile(XiT, n), tile(vb, n), start=True, stop=(n == 0))
                    if n > 0:
                        if n == 1:
                            pe.wait_ge(wt_ok, d + 1)
                        pe.wait_ge(s_ok, d * 3 + n)
                        last = mm(PS[5][:, 0:P], tile(nWT, n), S, start=False, stop=True)
                    last.then_inc(vn_ps, 1)
                    if n == 2:
                        ada_item(d, 3, par)
                    fill(20 + 2 * n, 21 + 2 * n)
                    if n == 0:
                        after(pe, ot_ok, d)
                        pe.wait_ge(qg_ok, d + 1)
                    else:
                        mm(tile(PS[7], n), S, tile(qg, n), start=True, stop=False)
                    pe.wait_ge(vn_ok, d * 4 + (n + 1))
                    last = mm(tile(PS[7], n), vnew[:, n % 2, :], tile(qkT, n), start=(n == 0), stop=True)
                    if n < NT - 1:
                        last = mm(PS[6][:, 0:P], tile(kdec_k, n), vnew[:, n % 2, :], start=True, stop=True)
                        last.then_inc(s_ps, 1)
                    else:
                        last.then_inc(o_ps, 1)
                    fill(21 + 2 * n, 22 + 2 * n)
                ada_item(d, 4, par)
                fill(28, 30)
                pe.wait_ge(osq_ok, d + 1)
                mm(PS[3][:], ones[:], osq, start=True, stop=True).then_inc(sso_ps, 1)
                fill(30, 32)

            def out_part(layer, w_sem, ready, fills):
                def fill(a, b):
                    for f in range(2 * (KD - 1) * a // fills, 2 * (KD - 1) * b // fills):
                        u, k = f // (KD - 1), f % (KD - 1)
                        if f == 0:
                            pe.wait_ge(ready, H - 1)
                            pe.wait_ge(w_sem[0], (layer + 1) * MIX_W)
                            out_banks_free(layer)
                        mm(PS[u][:], tile(OT[:, k, :], u), Wr[:, 0, k, :], start=(k == 0), stop=False)
                return fill

            def out_banks_free(layer):
                pe.wait_ge(ev_pj if layer == 0 else fev, 4 * H)

            project(0, 0, KD, 4 * KD)

            def step(s, slot):
                delta(s - 1, lambda a, b: project(s, slot, a, b), 1 - slot)

            step(1, 1)
            with pe.Fori(0, 3) as j:
                step(j * 2 + 2, 0)
                step(j * 2 + 3, 1)
            delta(H - 1, out_part(0, mix_w, ot_ok, 4 * KD), 1)
            pe.wait_ge(ada_rowok, ADA_FIRST + ADA_PER_HEAD * H)

            def out_projection(layer, w_sem, ready, ready_n):
                pe.wait_ge(ready, ready_n)
                base = layer * WO
                for nh in range(2):
                    pe.wait_ge(w_sem[nh], (layer + 1) * MIX_W)
                    for n in range(NT):
                        u = nh * NT + n
                        if u >= 2:
                            pe.wait_ge(wo_ok, base + u - 1)
                        for k in range(KD - 1 if u < 2 else 0, KD):
                            last = mm(PS[u % 2][:], tile(OT[:, k, :], n), Wr[:, nh, k, :], start=(k == 0), stop=(k == KD - 1))
                        last.then_inc(wo_ps, 1)
                        if u >= NT + 2:
                            norm_transposes(2 * layer + 1, u - NT - 2)
                for n in range(2):
                    narrow(2 * layer + 1, [n], routW[:, layer], NG + NE)
                    norm_transposes(2 * layer + 1, n + 2)
                narrow(2 * layer + 1, [2, 3], routW[:, layer], NG + NE).then_inc(r_ps, 1)

            def experts(i):
                m = M
                B = i * NE
                pe.wait_ge(r_both, 2 * i + 1)
                mm(PS[5][:, 0:(NT + 1) * NE], before[:], both, start=True, stop=False)
                for a in range(NT):
                    last = mm(PS[5][:, (a + 1) * NE:(NT + 1) * NE], ones[:],
                              both[:, a * NE:(a + 1) * NE].unsqueeze(1).to_broadcast([P, NT - a, NE]), start=False, stop=(a == NT - 1))
                last.then_inc(r_rank, 1)

                def slot_products(b):
                    pe.wait_ge(r_pos, NT * i + b + 1)
                    place = place1 if b % 2 == 0 else place2
                    for u in range(2 * NT):
                        last = mm(PS[5][:, 256 + b * NE:256 + (b + 1) * NE], place[:, u, :], ohd[u // NT][:, u % NT, :],
                                  start=(u == 0), stop=(u == 2 * NT - 1))
                    last.then_inc(slots_ps, 1)

                slot_products(0)

                def turn(u, n_in):
                    pe.wait_ge(m["xg"][u], n_in + 4 * B)
                    for k in range(KD):
                        last = tr(PS[2 + k // 4][:, (k % 4) * P:(k % 4) * P + P], xg[u][:, k * P:k * P + P], ident[:])
                    last.then_inc(m["xt_ps"], 1)

                def gate_up(e, u, slot, w_n):
                    pe.wait_ge(m["xt_a"], e + (B + 1))
                    pe.wait_ge(m["xt_b"], e + (B + 1))
                    pe.wait_ge(moe_w[slot], w_n * 16 + 4 * B)
                    for k in range(KD):
                        last = mm(PS[u][:], xgT[u][:, k, :], Wr[:, slot, k, :], start=(k == 0), stop=(k == KD - 1))
                    last.then_inc(m["gu_ps"], 1)

                def turn_act(e, u):
                    pe.wait_ge(m["ac"], e + (B + 1))
                    for k in range(2):
                        last = tr(tile(PS[4], k), ac[u][:, k * P:k * P + P], ident[:])
                    last.then_inc(m["at_ps"], 1)

                def down(e, u, w_n):
                    pe.wait_ge(m["at"], e + (B + 1))
                    pe.wait_ge(moe_d[u], w_n * 16 + 8 * B)
                    if not isinstance(e, int) or e > 0:
                        pe.wait_ge(m["ya"], e + B)
                        pe.wait_ge(m["yb"], e + B)
                    for nh in range(2):
                        for k in range(2):
                            last = mm(PS[6 + nh][:], acT[u][:, k, :],
                                      Dr[:, u, k * D + nh * 512:k * D + nh * 512 + 512], start=(k == 0), stop=(k == 1))
                    last.then_inc(m["dn_ps"], 1)

                turn(0, 16)
                gate_up(0, 0, 2, 1)
                pe.wait_ge(m["xt_a"], B + 1)
                turn(1, 16)

                def step(e, q, w_n, d_n, x_n, rows=True):
                    gate_up(e, q % 2, (q + 2) % 4, w_n)
                    turn_act(e - 1, (q + 1) % 2)
                    if rows:
                        turn((q + 1) % 4, x_n)
                    down(e - 1, (q + 1) % 2, d_n)

                for e in range(1, 5):
                    step(e, e % 4, e // 4 + 1, (e - 1) // 2 + 1, 16 * ((e + 1) // 4 + 1))
                    if e < NT:
                        slot_products(e)
                with pe.Fori(0, 6) as j:
                    for q in range(4):
                        e0 = 5 + q
                        step(j * 4 + e0, e0 % 4, j + (e0 // 4 + 1), j * 2 + ((e0 - 1) // 2 + 1),
                             (j + ((e0 + 1) // 4 + 1)) * 16)
                for e in range(29, NE):
                    step(e, e % 4, e // 4 + 1, (e - 1) // 2 + 1, 16 * ((e + 1) // 4 + 1), rows=(e < NE - 1))
                turn_act(NE - 1, 1)
                down(NE - 1, 1, NE // 2)

                xm = MX[i]
                pe.wait_ge(idx_ok, 2 * i + 2)
                n_x = pe.value_load(nextra[0:1, 0:1], min_val=0, max_val=MORE)
                with pe.If(n_x > 0):
                    with pe.Fori(0, n_x) as j:
                        pe.wait_ge(xm["moved"], j * 32 + 16)
                        for k in range(KD):
                            last = tr(PS[2 + k // 4][:, (k % 4) * P:(k % 4) * P + P], xg[0][:, k * P:k * P + P], ident[:])
                        last.then_inc(xm["stage"], 1)
                        pe.wait_ge(xm["stage"], stage_n("xt", j))
                        pe.wait_ge(xm["gu_w"], (j + 1) * 16)
                        for k in range(KD):
                            last = mm(PS[0][:], xgT[0][:, k, :], Wr[:, 2, k, :], start=(k == 0), stop=(k == KD - 1))
                        last.then_inc(xm["stage"], 1)
                        pe.wait_ge(xm["stage"], stage_n("ac", j))
                        for k in range(2):
                            last = tr(tile(PS[4], k), ac[0][:, k * P:k * P + P], ident[:])
                        last.then_inc(xm["stage"], 1)
                        pe.wait_ge(xm["stage"], stage_n("at", j))
                        pe.wait_ge(xm["dn_w"], (j + 1) * 16)
                        pe.wait_ge(m["ya"], B + NE)
                        pe.wait_ge(m["yb"], B + NE)
                        for nh in range(2):
                            for k in range(2):
                                last = mm(PS[6 + nh][:], acT[0][:, k, :],
                                          Dr[:, 0, k * D + nh * 512:k * D + nh * 512 + 512], start=(k == 0), stop=(k == 1))
                        last.then_inc(xm["stage"], 1)
                with pe.Else():
                    pe.nop()
                pe.wait_ge(m["ya"], B + NE)
                pe.wait_ge(m["yb"], B + NE)

            out_projection(0, mix_w, ot_ok, H)
            experts(0)

            for n in range(NT):
                norm_transposes(2, n)
                if n > 0:
                    narrow(2, [n - 1], fW, 2 * H)
            narrow(2, [NT - 1], fW, 2 * H).then_inc(decay_ps, 1)
            pe.wait_ge(decay_dve, 6)
            w16 = 2 * H
            mm(PS[5][:, 0:NT * w16], upto[:], lf, start=True, stop=False)
            for a in range(NT - 1):
                for n in range(a + 1, NT):
                    last = mm(PS[5][:, n * w16:(n + 1) * w16], ones[:], lf[:, a * w16:(a + 1) * w16],
                              start=False, stop=(a == NT - 2))
            last.then_inc(decay_ps, 1)

            def project_pair(p, slot, a, b):
                for f in range(a, b):
                    if f == 0:
                        pe.wait_ge(w_lo_pool, p * KD + 3 * KD)
                    if f < 16:
                        m, k = f // KD, f % KD
                        if m == 0 and isinstance(p, int) and p == 0:
                            pe.wait_ge(h_lo, KD + k + 1)
                        if k == 0:
                            after(pe, fev, p * 4 + (m - 1))
                        last = mm3(PS[m][:], Whi[:, slot * KD + k, m * P:m * P + P], Wlo[:, slot * KD + k, m * P:m * P + P],
                                   hHi[:, k, :], hLo[:, k, :], k)
                        if k == KD - 1:
                            last.then_inc(fpj_ps, 1)
                    else:
                        n, k = (f - 16) // KD, f % KD
                        if k == 0 and n % 2 == 0:
                            after(pe, fev, p * 4 + (n // 2 + 1))
                        last = mm3(PS[n // 2][:, (n % 2) * 256:(n % 2) * 256 + 256], tile(hHi[:, k, :], n), tile(hLo[:, k, :], n),
                                   Whi[:, slot * KD + k, 256:512], Wlo[:, slot * KD + k, 256:512], k)
                        if k == KD - 1 and n % 2 == 1:
                            last.then_inc(fpj_ps, 1)

            def attend(p, fill):
                fill(0, 3)
                pe.wait_ge(fev, p * 4 + 4)
                after(pe, ont_ok, p)
                after(pe, on_ok, p)
                mm(PS[7][:], halves[:], sqr[0], start=True, stop=True).then_inc(fs_ps, 1)
                mm(PS[6][:], halves[:], sqr[1], start=True, stop=True).then_inc(fs_ps, 1)
                fill(3, 4)
                for a in range(2):
                    if a == 0:
                        pe.wait_ge(nch_ok, p + 1)
                        pe.wait_ge(fr_ok, p * 2 + 1)
                    else:
                        pe.wait_ge(cb_ok, p * 2 + 1)
                    for n in range(NT):
                        last = mm(tile(PS[7], n), nch[:, a, n:n + 1].to_broadcast([P, P]), ident[:], start=True, stop=True)
                    last.then_inc(cb_ps, 1)
                    fill(4 + a, 5 + a)
                pe.wait_ge(qkh_ok, p * 2 + 2)

                def scores(u):
                    a, qt = u // NT, u % NT
                    w = (qt + 1) * P
                    after(pe, sc_ok, p * 8 + (u - 1))
                    mm(PS[2 + u % 2][:, 0:w], tile(qh, qt)[64 * a:64 * a + 64, :], kh[64 * a:64 * a + 64, 0:w],
                       start=True, stop=True).then_inc(sc_ps, 1)

                scores(0)
                for u in range(8):
                    a, qt = u // NT, u % NT
                    if u < 7:
                        scores(u + 1)
                    fill(6 + 4 * u, 8 + 4 * u)
                    pe.wait_ge(pr_ok, p * 8 + (u + 1))
                    n_free = p * 8 + (u - 1)
                    after(pe, pt_ok, n_free)
                    for n in range(qt + 1):
                        last = tr(tile(PS[4 + u % 2], n), tile(pS[u % 2], n), ident[:])
                    last.then_inc(pt_ps, 1)
                    fill(8 + 4 * u, 10 + 4 * u)
                    pe.wait_ge(pt_ok, p * 8 + (u + 1))
                    if u == 0:
                        pe.wait_ge(vs_ok, p + 1)
                        pe.wait_ge(fr_ok, p * 2 + 2)
                    for n in range(qt + 1):
                        last = mm(PS[6][:, qt * P + 64 * a:qt * P + 64 * a + 64], tile(pT[u % 2], n),
                                  vS[:, n, 64 * a:64 * a + 64], start=(n == 0), stop=(n == qt))
                    last.then_inc(pv_ps, 1)
                fill(38, 48)
                pe.wait_ge(on_ok, p + 1)
                for n in range(NT):
                    last = tr(tile(PS[7], n), on[:, n, :], ident[:])
                last.then_inc(ont_ps, 1)

            project_pair(0, 0, 0, 48)

            def pair_step(s, slot):
                attend(s - 1, lambda a, b: project_pair(s, slot, a, b))

            pair_step(1, 1)
            with pe.Fori(0, 3) as j:
                pair_step(j * 2 + 2, 0)
                pair_step(j * 2 + 3, 1)
            attend(H - 1, out_part(1, mix_w, ont_ok, 6 * KD))

            out_projection(1, mix_w, ont_ok, H)
            experts(1)

        @block.scalar
        def _(act):
            A = nc.scalar.activation
            link = Link(act, act_link)
            eps_ap, one_ap = eps_c[:, 0:1], eps_c[:, 1:2]

            def cp(dst, src):
                return nc.scalar.copy(dst, src)

            def log_exp_tables():
                nc.scalar.preload_act_table_set("natural_log_exp_and_others")

            def rsqrt(dst, src, scale, bias, tmp=None):
                tmp = dst if tmp is None else tmp
                link(A(tmp, src, ACT.Ln, bias=eps_ap[0:dst.shape[0]], scale=scale))
                return A(dst, tmp, ACT.Exp, bias=bias, scale=-0.5)

            def scaled_rows(phase, n):
                i = phase // 2 - 1
                act.wait_ge(y_in[n], 32 * (i + 1))
                nc.scalar.mul(Y[0][:, n, :], Y[0][:, n, :], w1[:, n:n + 1]).then_inc(y1_ok, 1)

            def weights_hi(slot, pieces):
                for k in pieces:
                    cp(Whi[:, slot * KD + k, :], Wr[:, slot, k, :]).then_inc(w_hi, 1)

            def h_parts(phase):
                act.wait_ge(n_h, 4 * phase + NT)
                if phase:
                    act.wait_ge(x_out, 16 * NT)
                act.wait_ge(n_tb, 4 * phase + NT)
                act.wait_ge(n_ta, 4 * phase + NT)
                for k in range(KD):
                    cp(hHi[:, k, :], hT[:, k, :]).then_inc(h_hi, 1)

            def rstd_tile(phase, n):
                link(A(sq_junk, X[:, n, :], ACT.Square, accum_out=ss[:, n:n + 1]))
                rsqrt(rstd[:, n:n + 1], ss[:, n:n + 1], 1.0 / D, 0.0, ss[:, n:n + 1]).then_inc(n_rs, 1)

            def norm(phase):
                for n in range(NT):
                    if phase in (2, 4):
                        if n == 0:
                            scaled_rows(phase, 0)
                        if n < NT - 1:
                            scaled_rows(phase, n + 1)
                    act.wait_ge(wo_ok, (phase - 1) // 2 * WO + (NT if phase % 2 else 2 * NT) + n + 1)
                    rstd_tile(phase, n)
                    if 0 < n and phase < 4:
                        take_tile(phase, n - 1)
                if phase < 4:
                    take_tile(phase, NT - 1)

            def take_tile(phase, n):
                act.wait_ge(n_tr, 4 * phase + n + 1)
                cp(hT[:, 0:4, n * P:n * P + P], PS[2 + 2 * (n % 2)][:].rearrange("p (k j) -> p k j", k=4)).then_inc(n_ta, 1)

            nc.scalar.preload_act_table(ACT.Silu)
            act.wait_ge(consts, 4)
            act.wait_ge(small_in, 16 * 11)
            act.wait_ge(cols_ok, 1)
            A(cact[:], cols[:, 96:104], ACT.Silu).then_inc(act_setup, 1)
            log_exp_tables()
            link(A(nega[:], nega[:], ACT.Exp))
            nc.scalar.mul(nega[:], nega[:], -1.0).then_inc(act_setup, 1)
            for a in range(ADA_FIRST):
                act.wait_ge(ada_ps, a + 1)
                to, col = (shiftB, a * ADA_W) if a < 4 else (scaleB, (a - 4) * ADA_W)
                A(to[:, col:col + ADA_W], PS[2 + a % 2][:, 0:ADA_W], ACT.Identity,
                  bias=0.0 if a < 4 else one_ap).then_inc(ada_rowok, 1)
                if a >= 4:
                    if a == 4:
                        act.wait_ge(x_in, 16)
                    rstd_tile(0, a - 4)
            act.wait_ge(mix_w[0], 64)
            weights_hi(0, range(KD))
            for n in range(NT):
                take_tile(0, n)
            h_parts(0)

            act.wait_ge(decay_dve, 1)
            link(A(t_ab2, t_ab2, ACT.Exp))
            link(A(t_ab2, t_ab2, ACT.Ln, bias=one_ap))
            A(beta, beta, ACT.Exp, scale=-1.0).then_inc(decay_act, 1)
            act.wait_ge(decay_dve, 3)
            link(A(nbeg, gc, ACT.Exp))
            link(A(kdecay, kdecay, ACT.Exp))
            A(egl, egl, ACT.Exp).then_inc(decay_act, 1)

            def take_product(s, m):
                act.wait_ge(proj_ps, s * 4 + (m + 1))
                if m == 2:
                    act.wait_ge(conv_ok, s * 3 + 1)
                else:
                    after(act, conv_ok, s * 3 + (-1 if m == 1 else 0))
                cp(cin[m % 2][:, CONV - 1:], PS[m % 2][:]).then_inc(ev_pj, 1)

            def squares(s):
                A(sqk, qkv[1], ACT.Square)
                A(sqq, qkv[0], ACT.Square).then_inc(sq_ok, 1)

            def delta(d, take, par, w_n=None):
                log_exp_tables()
                act.wait_ge(ss_ps, d * 2 + 1)
                rsqrt(sqk, PS[4][:], 1.0, 0.0).then_inc(rr_ok, 1)
                act.wait_ge(ss_ps, d * 2 + 2)
                rsqrt(sqq, PS[5][:], 1.0, eps_c[:, 2:3]).then_inc(rr_ok, 1)
                act.wait_ge(diff_ok, d + 1)
                A(egB, PS[2][:], ACT.Exp).then_inc(egb_ok, 1)
                act.wait_ge(msk_ok, d + 1)
                A(dT, dT, ACT.Exp).then_inc(dT_ok, 1)
                take(0)
                act.wait_ge(x1_ps, d + 1)
                cp(Xi, PS[5][:]).then_inc(x1_ok, 1)
                for l in range(1, LEVELS):
                    act.wait_ge(p_ps, d * 6 + l)
                    cp(Pp, PS[4][:]).then_inc(p_ok, 1)
                    if l == 4:
                        take(1)
                    if w_n is not None:
                        if l == 1:
                            act.wait_ge(mix_w[par], w_n * 64)
                        weights_hi(par, PIECES[l])
                    if l in ADA_LEVELS:
                        ada_item(d, ADA_LEVELS.index(l), par)
                act.wait_ge(wt_ps, d + 1)
                cp(nWT, PS[4][:]).then_inc(wt_ok, 1)
                for n in range(NT):
                    act.wait_ge(vn_ps, d * 4 + (n + 1))
                    cp(vnew[:, n % 2, :], PS[5][:, 0:P]).then_inc(vn_ok, 1)
                    if n == 2:
                        take(2)
                        ada_item(d, 3, par)
                act.wait_ge(o_ps, d + 1)
                A(osq, PS[7][:], ACT.Square).then_inc(osq_ok, 1)
                ada_item(d, 4, par)
                act.wait_ge(sso_ps, d + 1)
                rsqrt(rB, PS[3][:], 1.0 / P, 0.0).then_inc(ro_ok, 1)

            def ada_item(d, q, par):
                slot = (par + q) % 2
                act.wait_ge(ada_ps, d * 5 + (ADA_FIRST + q + 1))
                after(act, ada_out[slot], ada_stored(d, q, par))
                cp(ada_row[:, slot, :], PS[2][0:1, 0:ADA_W]).then_inc(ada_rowok, 1)
                act.wait_ge(ada_rowok, d * 5 + (ADA_FIRST + q + 1))
                layer, col = (0, (d * 2 + 8 + q) * ADA_W) if q < 2 else (1, (d * 3 + (q - 2)) * ADA_W)
                act.dma_start(ada_rows[layer:layer + 1, ds(col, ADA_W)], ada_row[:, slot, :]).then_inc(ada_out[slot], 16)

            def ada_stored(d, q, par):
                if isinstance(d, int):
                    return 16 * ((5 * d + q) // 2)
                return (d * 5 + (q - (par + q) % 2)) * 8

            def step(s, slot, w_n=None):
                delta(s - 1, lambda m: take_product(s, m), (slot + 1) % 2, w_n)
                end_of_step(s)

            def end_of_step(s):
                act.wait_ge(proj_ps, s * 4 + 4)
                after(act, ot_ok, s)
                A(gate_s, PS[1][:], ACT.Silu).then_inc(ev_pj, 1)
                act.wait_ge(conv_ok, s * 3 + 3)
                for m in range(3):
                    ins = A(qkv[m], qkv[m], ACT.Silu)
                link(ins)
                squares(s)

            for m in range(3):
                take_product(0, m)
                if m == 1:
                    act.wait_ge(mix_w[1], 64)
                    weights_hi(1, range(KD))
            end_of_step(0)
            step(1, 1, 2)
            with act.Fori(0, 2) as j:
                link.enter(j, 8)
                step(j * 2 + 2, 0, j + 2)
                step(j * 2 + 3, 1, j + 3)
                link.leave(2)
            step(6, 0, 4)
            step(7, 1)
            delta(7, lambda m: None, 1)

            def experts(i):
                m = M
                B = i * NE
                norm(2 * i + 1)
                act.wait_ge(r_both, 2 * i + 2)
                link(A(gidx, gidx, ACT.Exp))
                A(e21, e21, ACT.Exp).then_inc(r_e, 1)

                def rows(e, u):
                    act.wait_ge(m["xt_ps"], e + (B + 1))
                    if not isinstance(e, int) or e >= 2:
                        act.wait_ge(m["gu_ps"], e + (B - 1))
                    cp(xgT[u][:, 0:4, :], PS[2][:].rearrange("p (k j) -> p k j", k=4)).then_inc(m["xt_a"], 1)

                def silu(e, u):
                    act.wait_ge(m["gu_ps"], e + (B + 1))
                    if not isinstance(e, int) or e >= 2:
                        act.wait_ge(m["ac"], e + (B - 1))
                    A(sg[u], PS[u][:, 0:DE], ACT.Silu).then_inc(m["sg"], 1)

                def act_turned(e, u):
                    act.wait_ge(m["at_ps"], e + (B + 1))
                    if not isinstance(e, int) or e >= 2:
                        act.wait_ge(m["dn_ps"], e + (B - 1))
                    cp(acT[u], PS[4][:, 0:2 * P].rearrange("p (k j) -> p k j", k=2)).then_inc(m["at"], 1)

                def result(e, u, y_n):
                    act.wait_ge(m["dn_ps"], e + (B + 1))
                    if y_n is not None:
                        act.wait_ge(m["y"][u], y_n + 8 * B)
                    cp(yo[u][:, 0:512], PS[6][:]).then_inc(m["ya"], 1)

                rows(0, 0)
                rows(1, 1)

                def step(e, q, y_n, more=True):
                    silu(e, q % 2)
                    if not isinstance(e, int) or e >= 1:
                        act_turned(e - 1, (q + 1) % 2)
                        if more:
                            rows(e + 1, (q + 1) % 2)
                        result(e - 1, (q + 1) % 2, y_n)

                def y_free(e):
                    n = (e - 1) // 2
                    return 16 * n if n > 0 else None

                for e in range(0, 5):
                    step(e, e % 4, y_free(e) if e else None)
                with act.Fori(0, 6) as j:
                    for q in range(4):
                        e0 = 5 + q
                        step(j * 4 + e0, e0 % 4, (j * 2 + (e0 - 1) // 2) * 16)
                for e in range(29, NE):
                    step(e, e % 4, y_free(e), more=(e < NE - 1))
                act_turned(NE - 1, 1)
                result(NE - 1, 1, 16 * (NE // 2 - 1))

                log_exp_tables()
                xm = MX[i]
                act.wait_ge(idx_ok, 2 * i + 2)
                n_x = act.value_load(nextra[0:1, 0:1], min_val=0, max_val=MORE)
                with act.If(n_x > 0):
                    with act.Fori(0, n_x) as j:
                        act.wait_ge(xm["stage"], stage_n("gu_ps", j))
                        A(sg[0], PS[0][:, 0:DE], ACT.Silu).then_inc(xm["stage"], 1)
                        act.wait_ge(xm["stage"], stage_n("at_ps", j))
                        cp(acT[0], PS[4][:, 0:2 * P].rearrange("p (k j) -> p k j", k=2)).then_inc(xm["stage"], 1)
                with act.Else():
                    act.nop()
                act.nop()
                log_exp_tables()

            experts(0)

            norm(2)
            act.wait_ge(mix_w[0], MIX_W + 64)
            weights_hi(0, range(KD))
            h_parts(2)
            act.wait_ge(decay_dve, 5)
            link(A(tf2, tf2, ACT.Exp))
            A(tf2, tf2, ACT.Ln, bias=one_ap).then_inc(decay_act, 1)

            def take_pair(p, m):
                act.wait_ge(fpj_ps, p * 4 + (m + 1))
                if m < 2:
                    if m == 0:
                        after(act, qkh_ok, p * 2)
                    A(sqr[m], PS[m][:], ACT.Square)
                    ins = cp(qkr[m], PS[m][:])
                else:
                    ap = PS[m - 2][:].rearrange("p (n c) -> p n c", n=2)
                    lo = 2 * (m - 2)
                    if m == 2:
                        after(act, vs_ok, p)
                        after(act, sgt_ok, p)
                    cp(vraw[:, lo:lo + 2, :], ap[:, :, 0:P])
                    ins = A(eg[:, lo:lo + 2, :], ap[:, :, P:2 * P], ACT.Exp, scale=-1.0)
                ins.then_inc(fev, 1)

            def attend(p, take, par, w_n=None):
                act.wait_ge(fs_ps, p * 2 + 1)
                rsqrt(sqr[0], PS[7][:], 1.0 / 64, eps_c[:, 3:4]).then_inc(fr_ok, 1)
                act.wait_ge(fs_ps, p * 2 + 2)
                rsqrt(sqr[1], PS[6][:], 1.0 / 64, 0.0).then_inc(fr_ok, 1)
                for a in range(2):
                    act.wait_ge(cb_ps, p * 2 + (a + 1))
                    if a == 0:
                        after(act, cbt_ok, p * 2)
                    cp(cbS[:, a, :], PS[7][:]).then_inc(cb_ok, 1)
                for u in range(8):
                    qt = u % NT
                    w = (qt + 1) * P
                    act.wait_ge(sc_ok, p * 8 + (u + 1))
                    if u == 0:
                        after(act, on_ok, p)
                    n_free = p * 8 + (u - 1)
                    after(act, pt_ps, n_free)
                    A(pS[u % 2][:, 0:w], sS[u % 2][:, 0:w], ACT.Exp, bias=nmx[:, u:u + 1],
                      accum_out=rsum[:, u:u + 1]).then_inc(pr_ok, 1)
                    act.wait_ge(pt_ps, p * 8 + (u + 1))
                    after(act, pv_ps, n_free)
                    cp(pT[u % 2][:, 0:w], PS[4 + u % 2][:, 0:w]).then_inc(pt_ok, 1)
                    if u == 1:
                        take(0)
                    if u == 3:
                        take(1)
                    if u == 7:
                        take(2)
                    if w_n is not None:
                        if u == 0:
                            act.wait_ge(mix_w[par], MIX_W + w_n * 64)
                        weights_hi(par, (u,))
                act.wait_ge(ont_ps, p + 1)
                cp(OT[:, ds(p, 1), :].rearrange("p a t -> p (a t)"), PS[7][:]).then_inc(ont_ok, 1)
                take(3)

            for m in range(4):
                take_pair(0, m)
                if m == 1:
                    act.wait_ge(mix_w[1], MIX_W + 64)
                    weights_hi(1, range(KD))

            def pair_step(s, slot, w_n=None):
                attend(s - 1, lambda m: take_pair(s, m), 1 - slot, w_n)

            pair_step(1, 1, 2)
            with act.Fori(0, 2) as j:
                link.enter(j, 4)
                pair_step(j * 2 + 2, 0, j + 2)
                pair_step(j * 2 + 3, 1, j + 3)
                link.leave(2)
            pair_step(6, 0, 4)
            pair_step(7, 1)
            attend(7, lambda m: None, 1)
            experts(1)
            norm(4)

        @block.vector
        def _(dve):
            TT, TS, STT = nc.vector.tensor_tensor, nc.vector.tensor_scalar, nc.vector.scalar_tensor_tensor
            link = Link(dve, dve_link)
            cpv = nc.vector.tensor_copy

            dve.wait_ge(cols_ps, 1)
            cpv(cols[:], PS[0][:, 0:P]).then_inc(cols_ok, 1)
            dve.wait_ge(consts, 4)
            xi = hT[:, 0, 0:P].bitcast(I32)
            xj = hT[:, 0, P:2 * P].bitcast(I32)
            xl = hT[:, 1, 0:P].bitcast(I32)
            xf = hT[:, 2, 0:P]
            link(TT(xi, xi, xj, ALU.bitwise_xor))
            for l in range(LEVELS):
                link(TS(xl, xi, l, None, ALU.logical_shift_right))
                link(TS(xf, xl, 1.0, -1.0, ALU.is_equal, ALU.mult))
                link(TT(negmask[:, l, :], xf, before[:], ALU.mult))
            dve.wait_ge(cols_ok, 1)

            def scale_one(phase):
                dve.wait_ge(bc_in, 32 * phase)
                link(TS(scaleB[:], scaleB[:], 1.0, None, ALU.add))

            def h_tile(phase, n):
                dve.wait_ge(n_rs, 4 * phase + n + 1)
                if n >= 2:
                    dve.wait_ge(n_tr, 4 * phase + n - 1)
                    if phase % 2:
                        dve.wait_ge(hr_out[n % 2], 16 * (2 * (phase // 2) + n // 2))
                link(STT(out=hrow[n % 2], in0=X[:, n, :], scalar=rstd[:, n:n + 1], in1=scaleB[:], op0=ALU.mult, op1=ALU.mult))
                TT(hrow[n % 2], hrow[n % 2], shiftB[:], ALU.add).then_inc(n_h, 1)

            def take_tile(phase, n):
                dve.wait_ge(n_tr, 4 * phase + n + 1)
                cpv(hT[:, 4:8, n * P:n * P + P], PS[3 + 2 * (n % 2)][:].rearrange("p (k j) -> p k j", k=4)).then_inc(n_tb, 1)

            dve.wait_ge(ada_rowok, ADA_FIRST)
            for n in range(NT):
                h_tile(0, n)
                if n > 0:
                    take_tile(0, n - 1)
            take_tile(0, NT - 1)

            def h_parts(phase):
                for k in range(KD):
                    dve.wait_ge(h_hi, phase // 2 * KD + k + 1)
                    TT(hLo[:, k, :], hT[:, k, :], hHi[:, k, :], ALU.subtract).then_inc(h_lo, 1)

            hn = lambda ap: ap.rearrange("p (h n) -> p n h", h=H)
            dve.wait_ge(decay_ps, 1)
            ab = PS[6][:, 0:NT * 2 * H].rearrange("p (n c) -> p n c", n=NT)
            link(TT(hn(t_ab), ab[:, :, 0:H], dtb[:].unsqueeze(1).to_broadcast([P, NT, H]), ALU.add))
            link(TS(t_ab2, t_ab, -1.0, None, ALU.mult))
            TT(t_ab2, t_ab2, t_ab, ALU.min)
            cpv(hn(beta), ab[:, :, H:2 * H]).then_inc(decay_dve, 1)
            h_parts(0)
            dve.wait_ge(decay_act, 1)
            link(STT(out=la, in0=t_ab, scalar=0.0, in1=t_ab2, op0=ALU.max, op1=ALU.add))
            dve.wait_ge(act_setup, 2)
            link(TT(hn(la), hn(la), nega[:].unsqueeze(1).to_broadcast([P, NT, H]), ALU.mult))
            link(TS(beta, beta, 1.0, None, ALU.add))
            nc.vector.reciprocal(beta, beta).then_inc(decay_dve, 1)
            dve.wait_ge(decay_ps, 2)
            link(cpv(gc, PS[5][:, 0:32]))
            link(cpv(egl, PS[5][:, 32:64]))
            TT(kdecay, egl, gc, ALU.subtract).then_inc(decay_dve, 1)
            dve.wait_ge(decay_act, 2)
            STT(out=nbeg, in0=nbeg, scalar=-1.0, in1=beta, op0=ALU.mult, op1=ALU.mult).then_inc(decay_dve, 1)
            dve.wait_ge(decay_dve, 4)

            def hcol(ap, d):
                return over(ap[:, ds(d * NT, NT)])

            def conv(s, m, taps_now=range(CONV)):
                src = cin[m % 2]
                for j in taps_now:
                    tap = taps[:, j * 3 + m:j * 3 + m + 1]
                    if j == 0:
                        dve.wait_ge(row_ok, s + 1)
                        dve.wait_ge(ev_pj, s * 4 + (m + 1))
                        link(TS(qkv[m], src[:, 0:T], tap, None, ALU.mult))
                    else:
                        ins = STT(out=qkv[m], in0=src[:, j:j + T], scalar=tap, in1=qkv[m], op0=ALU.mult, op1=ALU.add)
                        if j < CONV - 1:
                            link(ins)
                        else:
                            ins.then_inc(conv_ok, 1)

            def ada_item(d, par):
                if isinstance(d, int):
                    dve.wait_ge(ada_in[par], 32 * ((5 * d) // 2 + 1))
                else:
                    dve.wait_ge(ada_in[par], (d * 5 + (2 - par)) * 16)
                dve.wait_ge(ada_ps, d * 5 + (ADA_FIRST - 1))
                w = Dr[:, par, :].rearrange("p (k n) -> p k n", k=KD)
                for k in range(KD):
                    ins = STT(out=ada_acc[:, par, :], in0=w[:, k, :], scalar=cact[:, k:k + 1],
                              in1=bias_row[:, par, :] if k == 0 else ada_acc[:, par, :], op0=ALU.mult, op1=ALU.add)
                    if k < KD - 1:
                        link(ins)
                    else:
                        ins.then_inc(ada_dve, 1)

            def delta(d, s, par, split=True):
                after(dve, ot_ok, d)
                dve.wait_ge(gb_ps, d + 1)
                TT(t4(dT), t4(PS[2][:]), hcol(gc, d), ALU.subtract).then_inc(diff_ok, 1)
                ada_item(d, par)
                dve.wait_ge(rr_ok, d * 2 + 1)
                TT(khat, qkv[1], sqk, ALU.mult)
                dve.wait_ge(rr_ok, d * 2 + 2)
                TT(qhat, qkv[0], sqq, ALU.mult).then_inc(hat_ok, 1)
                dve.wait_ge(hat_ok, d + 1)
                TT(kb, khat, PS[3][:], ALU.mult).then_inc(kb_ok, 1)
                dve.wait_ge(egb_ok, d + 1)
                TT(qg, qhat, egB, ALU.mult).then_inc(qg_ok, 1)
                dve.wait_ge(v_ps, d + 1)
                TT(t4(vb), t4(PS[6][:]), hcol(beta, d), ALU.mult).then_inc(vb_ok, 1)
                dve.wait_ge(k_ps, d + 1)
                TT(t4(kwn), t4(PS[2][:]), hcol(nbeg, d), ALU.mult)
                TT(t4(kdec_k), t4(PS[2][:]), hcol(kdecay, d), ALU.mult).then_inc(kd_ok, 1)
                dve.wait_ge(kk_ps, d + 1)
                dve.wait_ge(dT_ok, d + 1)
                TT(aT, PS[3][:], dT, ALU.mult).then_inc(at_ok, 1)
                dve.wait_ge(at_ok, d + 1)
                link(TT(t4(nt[0]), t4(aT), negmask[:, 0:1, :].to_broadcast([P, NT, P]), ALU.mult))
                TT(t4(XiT), t4(nt[0]), ident[:].unsqueeze(1).to_broadcast([P, NT, P]), ALU.add).then_inc(xt_ok, 1)
                dve.wait_ge(qk_ps, d + 1)
                TT(qkT, PS[4][:], dT, ALU.mult).then_inc(qkt_ok, 1)
                for l in range(1, LEVELS):
                    lv = d * (2 * LEVELS - 3) + 2 * l
                    if l < LEVELS - 1:
                        dve.wait_ge(lv_ps, lv - 1)
                        TT(Xi, Xi, PS[5][:], ALU.add).then_inc(lv_ok, 1)
                    dve.wait_ge(lv_ps, lv if l < LEVELS - 1 else lv - 1)
                    TT(XiT, XiT, PS[6][:], ALU.add).then_inc(lv_ok, 1)
                    for k in PIECES[l] if split else ():
                        dve.wait_ge(w_hi, d * KD + (2 * KD + k + 1))
                        at = ds((d % 2) * KD + k, 1)
                        TT(Wlo[:, at, :], Wr[:, 0:2].rearrange("p s k n -> p (s k) n")[:, at, :], Whi[:, at, :],
                           ALU.subtract).then_inc(w_lo, 1)
                    if s is not None and l in (2, 3):
                        conv(s, 0, (2 * l - 4, 2 * l - 3))
                    if s is not None and l in (5, 6):
                        conv(s, 1, (2 * l - 10, 2 * l - 9))
                for n in range(NT - 1):
                    dve.wait_ge(s_ps, d * 3 + (n + 1))
                    if n == 0:
                        cpv(S, PS[6][:, 0:P]).then_inc(s_ok, 1)
                    else:
                        dve.wait_ge(s_ok, d * 3 + n)
                        STT(out=S, in0=S, scalar=egl[:, ds(d * NT + n, 1)], in1=PS[6][:, 0:P],
                            op0=ALU.mult, op1=ALU.add).then_inc(s_ok, 1)
                if s is not None:
                    conv(s, 2)
                dve.wait_ge(ro_ok, d + 1)
                link(STT(out=t1, in0=PS[7][:], scalar=cols[:, 104:105], in1=rB, op0=ALU.mult, op1=ALU.mult))
                TT(OT[:, ds(d, 1), :].rearrange("p a t -> p (a t)"), t1, gate_s, ALU.mult).then_inc(ot_ok, 1)

            for m in range(3):
                conv(0, m)
            delta(0, 1, 0)
            with dve.Fori(0, 2) as j:
                link.enter(j, 2 * (2 + 3 * (CONV - 1) + KD - 1))
                delta(j * 2 + 1, j * 2 + 2, 1)
                delta(j * 2 + 2, j * 2 + 3, 0)
                link.leave(2)
            delta(H - 3, H - 2, 1)
            delta(H - 2, H - 1, 0, split=False)
            delta(H - 1, None, 1, split=False)

            def out_projection(layer):
                phase = 2 * layer + 1
                dve.wait_ge(x_back, 16 * (layer + 1))
                dve.wait_ge(gate_in, 16 * (2 * layer + 1))
                scale_one(phase)
                for u in range(2 * NT):
                    nh, n = u // NT, u % NT
                    cs = slice(nh * 512, nh * 512 + 512)
                    dve.wait_ge(wo_ps, layer * 2 * NT + u + 1)
                    if u > 0:
                        dve.wait_ge(wo_ok, layer * WO + u)
                    link(TT(ymul, PS[u % 2][:], gateB[:, cs], ALU.mult))
                    TT(X[:, n, cs], X[:, n, cs], ymul, ALU.add).then_inc(wo_ok, 1)
                    if u > NT:
                        h_tile(phase, u - NT - 1)
                    if u == 2 * NT - 1:
                        take_tile(phase, 0)
                take_tile(phase, 1)
                h_tile(phase, NT - 1)
                for n in range(2, NT):
                    take_tile(phase, n)

            def route(i):
                red = nc.vector.tensor_reduce
                b4 = lambda ap, w: ap.unsqueeze(2).to_broadcast([P, NT, w])
                iot = lambda w: iota_e[:, 0:w].unsqueeze(1).to_broadcast([P, NT, w])
                dve.wait_ge(r_ps, i + 1)
                link(TT(lg, PS[6][:, 0:NT * (NG + NE)].rearrange("p (n c) -> p n c", n=NT),
                        routB[:, i, :].unsqueeze(1).to_broadcast([P, NT, NG + NE]), ALU.add))
                grp, exp_l = lg[:, :, 0:NG], lg[:, :, NG:]

                def first_max(src, w, mval, onehot, scratch):
                    link(red(mval, src, AX_X, ALU.max))
                    link(TT(scratch, src, b4(mval, w), ALU.is_equal))
                    link(STT(out=scratch, in0=scratch, scalar=-1000.0, in1=iot(w), op0=ALU.mult, op1=ALU.add))
                    link(red(mi, scratch, AX_X, ALU.min))
                    link(TT(onehot, scratch, b4(mi, w), ALU.is_equal))

                first_max(grp, NG, gm, geq, gidx)
                link(TT(gidx, grp, b4(gm, NG), ALU.subtract))
                g_of = geq.unsqueeze(3).to_broadcast([P, NT, NG, EPG])
                e4 = lambda ap: ap.rearrange("p n (g e) -> p n g e", g=NG)
                link(TT(e4(el), e4(exp_l), g_of, ALU.mult))
                link(TS(e4(tmp32), g_of, -NEG, NEG, ALU.mult, ALU.add))
                link(TT(el, el, tmp32, ALU.add))
                first_max(el, NE, m1, oh1, tmp32)
                link(STT(out=el, in0=oh1, scalar=4 * NEG, in1=el, op0=ALU.mult, op1=ALU.add))
                first_max(el, NE, m2, oh2, tmp32)
                TS(both[:, NT * NE:], oh1[:, 0, :], 0.0, None, ALU.mult)
                TT(both[:, 0:NT * NE].rearrange("p (n e) -> p n e", n=NT), oh1, oh2, ALU.add).then_inc(r_both, 1)
                TT(e21, m2, m1, ALU.subtract).then_inc(r_both, 1)
                dve.wait_ge(r_e, i + 1)
                link(red(gz, gidx, AX_X, ALU.add))
                link(nc.vector.reciprocal(gp, gz))
                link(TS(w1, e21, 1.0, None, ALU.add))
                link(nc.vector.reciprocal(w1, w1))
                link(TT(w1, w1, gp, ALU.mult))
                link(TT(w2, w1, e21, ALU.mult))
                for k, oh in enumerate((oh1, oh2)):
                    link(TT(ohd[k], oh, b4(dest1[:, k, :], NE), ALU.mult))
                dve.wait_ge(r_rank, i + 1)
                for k, oh in enumerate((oh1, oh2)):
                    link(TT(tmp32, PS[5][:, 0:NT * NE].rearrange("p (n e) -> p n e", n=NT), oh, ALU.mult))
                    link(red(posf[:, k, :], tmp32, AX_X, ALU.add))
                place_slots(i, 0)
                slot_table(i, 0, 1)

            def place_slots(i, b):
                if b > 0:
                    dve.wait_ge(r_pos, NT * i + b)
                    link(TS(posb, posf, -float(b * P), None, ALU.add))
                if b >= 2:
                    dve.wait_ge(slots_ps, NT * i + b - 1)
                place = place1 if b % 2 == 0 else place2
                for u in range(2 * NT):
                    ins = TS(place[:, u, :], iota_r[:], (posb if b else posf)[:, u // NT, u % NT:u % NT + 1], None, ALU.is_equal)
                ins.then_inc(r_pos, 1)

            def further_items(i):
                red = nc.vector.tensor_reduce
                slot_table(i, 1, NT)
                cnt = PS[5][:, NT * NE:(NT + 1) * NE]
                link(TS(over_n, cnt, P + 0.5, None, ALU.is_gt))
                for b in range(2, NT):
                    link(STT(out=over_n, in0=cnt, scalar=b * P + 0.5, in1=over_n, op0=ALU.is_gt, op1=ALU.add))
                row, col = iota_e[:].unsqueeze(2).to_broadcast([P, NE, NE]), iota_e[:].unsqueeze(1).to_broadcast([P, NE, NE])
                link(TT(lt, col, row, ALU.is_lt))
                link(TT(lt, lt, over_n.unsqueeze(1).to_broadcast([P, NE, NE]), ALU.mult))
                link(red(before_n, lt, AX_X, ALU.add))
                wide = lambda ap: ap.unsqueeze(1).to_broadcast([P, MORE, NE])
                link(TT(item_d, iota_e[:, 0:MORE].unsqueeze(2).to_broadcast([P, MORE, NE]), wide(before_n), ALU.subtract))
                link(TT(item_s, item_d, wide(over_n), ALU.is_lt))
                link(STT(out=item_s, in0=item_d, scalar=-0.5, in1=item_s, op0=ALU.is_gt, op1=ALU.mult))
                link(TT(item_v, item_s, wide(iota_e[:]), ALU.mult))
                link(red(item_f[:, 0, :], item_v, AX_X, ALU.add))
                link(TT(item_v, item_s, item_d, ALU.mult))
                link(red(item_f[:, 1, :], item_v, AX_X, ALU.add))
                link(TS(item_f[:, 2, :], item_f[:, 1, :], float(NE), float(NE), ALU.mult, ALU.add))
                link(TT(item_f[:, 1, :], item_f[:, 2, :], item_f[:, 0, :], ALU.add))
                link(red(mi[:, 0:1], over_n, AX_X, ALU.add))
                cpv(nextra, mi[:, 0:1])
                cpv(item_i, item_f[:, 0:2, :].rearrange("p a j -> p (a j)")).then_inc(idx_ok, 1)

            def slot_table(i, b0, b1):
                cs = slice(b0 * NE, b1 * NE)
                dve.wait_ge(slots_ps, NT * i + b1)
                link(TS(slot_t[:, cs], PS[5][:, 256 + b0 * NE:256 + b1 * NE], 0.5, float(NO_ROW), ALU.is_lt, ALU.mult))
                link(STT(out=slot_f[:, cs], in0=PS[5][:, 256 + b0 * NE:256 + b1 * NE], scalar=-1.0, in1=slot_t[:, cs], op0=ALU.add, op1=ALU.add))
                cpv(slot_i[:, cs], slot_f[:, cs])
                link(TS(slot_t[:, cs], slot_f[:, cs], T - 0.5, float(-T), ALU.is_ge, ALU.mult))
                ins = TT(slot_g[:, cs], slot_f[:, cs], slot_t[:, cs], ALU.add)
                if b0 == 0:
                    ins.then_inc(idx_ok, 1)
                else:
                    link(ins)

            def experts(i):
                m = M
                B = i * NE

                def rows(e, u):
                    dve.wait_ge(m["xt_ps"], e + (B + 1))
                    if not isinstance(e, int) or e >= 2:
                        dve.wait_ge(m["gu_ps"], e + (B - 1))
                    cpv(xgT[u][:, 4:8, :], PS[3][:].rearrange("p (k j) -> p k j", k=4)).then_inc(m["xt_b"], 1)

                def product(e, u):
                    dve.wait_ge(m["sg"], e + (B + 1))
                    if not isinstance(e, int) or e >= 2:
                        dve.wait_ge(m["at_ps"], e + (B - 1))
                    TT(ac[u], sg[u], PS[u][:, DE:2 * DE], ALU.mult).then_inc(m["ac"], 1)

                def result(e, u, y_n):
                    dve.wait_ge(m["dn_ps"], e + (B + 1))
                    if y_n is not None:
                        dve.wait_ge(m["y"][u], y_n + 8 * B)
                    cpv(yo[u][:, 512:D], PS[7][:]).then_inc(m["yb"], 1)

                def step(e, q, y_n, more=True):
                    product(e, q % 2)
                    if not isinstance(e, int) or e >= 1:
                        if more:
                            rows(e + 1, (q + 1) % 2)
                        result(e - 1, (q + 1) % 2, y_n)

                rows(0, 0)
                rows(1, 1)
                for e in range(0, 5):
                    step(e, e % 4, 16 * ((e - 1) // 2) if e > 2 else None)
                    if e < NT - 1:
                        place_slots(i, e + 1)
                further_items(i)
                with dve.Fori(0, 6) as j:
                    for q in range(4):
                        e0 = 5 + q
                        step(j * 4 + e0, e0 % 4, (j * 2 + (e0 - 1) // 2) * 16)
                for e in range(29, NE):
                    step(e, e % 4, 16 * ((e - 1) // 2), more=(e < NE - 1))
                result(NE - 1, 1, 16 * (NE // 2 - 1))

                xm = MX[i]
                dve.wait_ge(idx_ok, 2 * i + 2)
                n_x = dve.value_load(nextra[0:1, 0:1], min_val=0, max_val=MORE)
                with dve.If(n_x > 0):
                    with dve.Fori(0, n_x) as j:
                        dve.wait_ge(xm["stage"], stage_n("xt_ps", j))
                        cpv(xgT[0][:, 0:4, :], PS[2][:].rearrange("p (k j) -> p k j", k=4))
                        cpv(xgT[0][:, 4:8, :], PS[3][:].rearrange("p (k j) -> p k j", k=4)).then_inc(xm["stage"], 1)
                        dve.wait_ge(xm["stage"], stage_n("sg", j))
                        TT(ac[0], sg[0], PS[0][:, DE:2 * DE], ALU.mult).then_inc(xm["stage"], 1)
                        dve.wait_ge(xm["stage"], stage_n("dn_ps", j))
                        dve.wait_ge(m["y"][0], 8 * B + 16 * (NE // 2))
                        cpv(yo[0][:, 0:512], PS[6][:])
                        cpv(yo[0][:, 512:D], PS[7][:]).then_inc(xm["stage"], 1)
                with dve.Else():
                    dve.nop()
                dve.nop()

            def combine(i):
                phase = 2 * i + 2
                dve.wait_ge(gate_in, 16 * (2 * i + 2))
                if phase < 4:
                    scale_one(phase)
                else:
                    dve.wait_ge(bc_in, 3 * 32 + 16)
                for n in range(NT):
                    dve.wait_ge(y1_ok, NT * i + n + 1)
                    link(STT(out=Y[1][:, n, :], in0=Y[1][:, n, :], scalar=w2[:, n:n + 1], in1=Y[0][:, n, :], op0=ALU.mult, op1=ALU.add))
                    link(TT(Y[1][:, n, :], Y[1][:, n, :], gateB[:], ALU.mult))
                    TT(X[:, n, :], X[:, n, :], Y[1][:, n, :], ALU.add).then_inc(wo_ok, 1)
                    if n > 0:
                        finish_tile(phase, n - 1)
                finish_tile(phase, NT - 1)
                if phase < 4:
                    take_tile(phase, NT - 1)

            def finish_tile(phase, n):
                if phase < 4:
                    h_tile(phase, n)
                    if n > 0:
                        take_tile(phase, n - 1)
                else:
                    dve.wait_ge(n_rs, 4 * phase + n + 1)
                    STT(out=X[:, n, :], in0=X[:, n, :], scalar=rstd[:, n:n + 1], in1=shiftB[:], op0=ALU.mult, op1=ALU.mult).then_inc(fin_ok, 1)

            out_projection(0)
            route(0)
            experts(0)
            combine(0)

            dve.wait_ge(decay_ps, 3)
            link(TT(tf1.rearrange("p (n c) -> p n c", n=NT), PS[6][:, 0:NT * 2 * H].rearrange("p (n c) -> p n c", n=NT),
                    bfb[:].unsqueeze(1).to_broadcast([P, NT, 2 * H]), ALU.add))
            link(TS(tf2, tf1, -1.0, None, ALU.mult))
            TT(tf2, tf2, tf1, ALU.min).then_inc(decay_dve, 1)
            h_parts(2)
            dve.wait_ge(decay_act, 3)
            STT(out=lf, in0=tf1, scalar=0.0, in1=tf2, op0=ALU.min, op1=ALU.subtract).then_inc(decay_dve, 1)
            dve.wait_ge(decay_ps, 4)
            TS(cumn.rearrange("p (c n) -> p n c", c=2 * H), PS[5][:, 0:NT * 2 * H].rearrange("p (n c) -> p n c", n=NT),
               -1.0, None, ALU.mult).then_inc(decay_dve, 1)

            def attend(p):
                dve.wait_ge(fev, p * 4 + 4)
                after(dve, on_ok, p)
                link(TS(eg, eg, 1.0, None, ALU.add))
                nc.vector.reciprocal(sgate, eg).then_inc(sgt_ok, 1)
                dve.wait_ge(fr_ok, p * 2 + 1)
                STT(out=qh, in0=qkr[0], scalar=cols[:, 105:106], in1=sqr[0], op0=ALU.mult, op1=ALU.mult).then_inc(qkh_ok, 1)
                dve.wait_ge(fr_ok, p * 2 + 2)
                STT(out=kh, in0=qkr[1], scalar=cols[:, 106:107], in1=sqr[1], op0=ALU.mult, op1=ALU.mult).then_inc(qkh_ok, 1)
                for u in range(8):
                    a, qt = u // NT, u % NT
                    w = (qt + 1) * P
                    dve.wait_ge(sc_ps, p * 8 + (u + 1))
                    if qt == 0:
                        dve.wait_ge(cbt_ok, p * 2 + (a + 1))
                    after(dve, pr_ok, p * 8 + (u - 1))
                    dve.sem_inc(dve_passed, 1)
                    link(nc.vector.tensor_tensor_reduce(out=sS[u % 2][:, 0:w], in0=PS[2 + u % 2][:, 0:w],
                                                        in1=cbT[a][:, offs[qt]:offs[qt] + w], scale=1.0, scalar=3 * NEG,
                                                        op0=ALU.add, op1=ALU.max, accum_out=mx[:, u:u + 1]))
                    if u == 0:
                        after(dve, pr_ok, p * 8)
                    TS(nmx[:, u:u + 1], mx[:, u:u + 1], -1.0, None, ALU.mult).then_inc(sc_ok, 1)
                dve.wait_ge(pr_ok, p * 8 + 8)
                link(nc.vector.reciprocal(rinv, rsum))
                dve.wait_ge(pv_ps, p * 8 + 8)
                after(dve, ont_ps, p)
                ri = rinv.rearrange("p (a n) -> p n a", a=2).unsqueeze(3).to_broadcast([P, NT, 2, 64])
                link(TT(on.rearrange("p n (a c) -> p n a c", a=2), PS[6][:].rearrange("p (n a c) -> p n a c", n=NT, a=2), ri, ALU.mult))
                TT(on, on, sgate, ALU.mult).then_inc(on_ok, 1)

            attend(0)
            with dve.Fori(1, H) as p:
                link.enter(p - 1, 11)
                attend(p)
                link.leave(H - 1)

            out_projection(1)
            route(1)
            experts(1)
            combine(1)

        @block.gpsimd
        def _(pool):
            g = nc.gpsimd
            link = Link(pool, pool_link, pool_passed)

            def passed():
                pool.sem_inc(pool_passed, 1)

            g.memset(rows_in[:], 0.0)
            g.memset(bias_row[:], 0.0).then_inc(consts, 1)
            g.memset(ones[:], 1.0)
            link(g.memset(ident[:], 0.0))
            sel = g.affine_select
            sel(out=ident[:], in_=ident[:], pattern=[[-1, P]], compare_op=ALU.not_equal, fill=1.0, base=0, channel_multiplier=1)
            sel(out=upto[:], in_=ones[:], pattern=[[1, P]], compare_op=ALU.is_ge, fill=0.0, base=0, channel_multiplier=-1).then_inc(consts, 1)
            sel(out=before[:], in_=ones[:], pattern=[[1, P]], compare_op=ALU.is_ge, fill=0.0, base=-1, channel_multiplier=-1)
            link(g.memset(halves[:], 0.0))
            g.memset(halves[0:64, 0:64], 1.0)
            g.memset(halves[64:P, 64:P], 1.0).then_inc(consts, 1)
            pool.wait_ge(consts, 3)
            g.memset(eps_c[:, 0:1], EPS)
            g.memset(eps_c[:, 1:2], 1.0)
            g.memset(eps_c[:, 2:3], float(np.log(P ** -0.5)))
            g.memset(eps_c[:, 3:4], float(np.log(64 ** -0.5)))
            g.iota(hT[:, 0, 0:P].bitcast(I32), pattern=[[1, P]], base=0, channel_multiplier=0)
            g.iota(hT[:, 0, P:2 * P].bitcast(I32), pattern=[[0, P]], base=0, channel_multiplier=1)
            g.iota(hT[:, 3, 0:2 * NT].bitcast(I32), pattern=[[T, 2], [P, NT]], base=1, channel_multiplier=1)
            link(g.iota(iota_i[:], pattern=[[1, NE]], base=0, channel_multiplier=0))
            g.tensor_copy(iota_e[:], iota_i[:])
            g.tensor_copy(iota_r[:], hT[:, 0, 0:P].bitcast(I32))
            g.tensor_copy(dest1[:].rearrange("p k n -> p (k n)"), hT[:, 3, 0:2 * NT].bitcast(I32)).then_inc(consts, 1)
            pool.wait_ge(consts, 4)

            def weights_lo(slot, n, pieces=range(KD)):
                for k in pieces:
                    pool.wait_ge(w_hi, n + (k + 1))
                    at = ds(slot * KD + k, 1)
                    if not isinstance(slot, int):
                        passed()
                    g.tensor_tensor(Wlo[:, at, :], Wr[:, 0:2].rearrange("p s k n -> p (s k) n")[:, at, :], Whi[:, at, :],
                                    ALU.subtract).then_inc(w_lo_pool, 1)

            weights_lo(0, 0)
            pool.wait_ge(decay_dve, 4)
            for u in range(2):
                g.memset(cin[u][:, 0:CONV - 1], 0.0)

            def head_rows(s):
                after(pool, conv_ok, s * 3)
                if not isinstance(s, int):
                    passed()
                g.tensor_copy(taps[:].unsqueeze(2), cols[:, 0:3 * CONV * KD].rearrange("p (c h) -> p c h", h=KD)[:, :, ds(s, 1)])
                g.tensor_copy(lah[:, 0, :], la[:, ds(s * NT, NT)])
                g.tensor_copy(lah[:, 1, :], beta[:, ds(s * NT, NT)]).then_inc(row_ok, 1)

            def ada_item(d, q, par):
                slot = (par + q) % 2
                if isinstance(d, int):
                    n_in = 32 * ((5 * d + q) // 2 + 1)
                else:
                    n_in = (d * 5 + (q + 2 - slot)) * 16
                pool.wait_ge(ada_in[slot], n_in)
                passed()
                after(pool, ada_ps, d * 5 + (ADA_FIRST + q - 1))
                passed()
                w = Dr[:, slot, :].rearrange("p (k n) -> p k n", k=KD)
                link(g.tensor_tensor(w, w, cact[:].unsqueeze(2).to_broadcast([P, KD, ADA_W]), ALU.mult))
                for half in (4, 2, 1):
                    link(g.tensor_tensor(w[:, 0:half], w[:, 0:half], w[:, half:2 * half], ALU.add))
                ins = g.tensor_tensor(ada_acc[:, slot, :], w[:, 0, :], bias_row[:, slot, :], ALU.add)
                ins.then_inc(ada_pool, 1)

            def delta(d, s, par):
                pool.wait_ge(diff_ok, d + 1)
                passed()
                g.affine_select(out=t4(dT), in_=t4(dT), pattern=[[0, NT], [1, P]], compare_op=ALU.is_ge, fill=NEG,
                                base=0, channel_multiplier=-1).then_inc(msk_ok, 1)
                ada_item(d, 1, par)
                pool.wait_ge(at_ok, d + 1)
                for l in range(1, LEVELS):
                    if l == LEVELS - 1:
                        pool.wait_ge(qk_ps, d + 1)
                        passed()
                    g.tensor_tensor(t4(nt[l]), t4(aT), negmask[:, l:l + 1, :].to_broadcast([P, NT, P]), ALU.mult).then_inc(nt_ok, 1)
                if s is not None:
                    head_rows(s)
                ada_item(d, 2, par)
                ada_item(d, 3, par)
                ada_item(d, 4, par)

            pool.wait_ge(cols_ok, 1)
            pool.wait_ge(act_setup, 1)
            head_rows(0)
            weights_lo(1, KD)
            delta(0, 1, 0)
            with pool.Fori(0, 3) as j:
                link.enter(j, 2 * (ADA_PER_HEAD - 1) * 4)
                delta(j * 2 + 1, j * 2 + 2, 1)
                delta(j * 2 + 2, j * 2 + 3, 0)
                link.leave(3)
            delta(7, None, 1)

            def experts(i):
                m = M
                B = i * NE
                rows_of = h_rows[i]
                pool.wait_ge(wo_ps, (i + 1) * 2 * NT)
                for u in range(4):
                    ins = g.memset(xg[u], 0.0)
                link(ins)
                pool.wait_ge(idx_ok, 2 * i + 1)
                for u in range(2):
                    pool.wait_ge(hr_out[u], 16 * 2 * (i + 1))

                def gather(e, u):
                    g.indirect_dma_start(out=xg[u], out_offset=None, in_=rows_of,
                                         in_offset=bass.IndirectOffsetOnAxis(ap=gidx_i[:, u, :], axis=0),
                                         bounds_check=T - 1, oob_is_err=False).then_inc(m["xg"][u], 16)

                def pick(e, u):
                    g.tensor_copy(gidx_i[:, u, :], slot_g[:, ds(e, 1)]).then_inc(m["cp"], 1)

                def scatter(e, u):
                    g.indirect_dma_start(out=y_rows[i], out_offset=bass.IndirectOffsetOnAxis(ap=sidx[:, u, :], axis=0),
                                         in_=yo[u], in_offset=None, bounds_check=2 * T - 1,
                                         oob_is_err=False).then_inc(m["y"][u], 16)

                for e in range(4):
                    pick(e, e)
                    pool.wait_ge(m["cp"], 2 * B + e + 1)
                    gather(e, e)

                def step(e, q, cp_n, y_n, more=True):
                    u = q % 2
                    if more:
                        pool.wait_ge(m["xt_ps"], e + (B + 1))
                        passed()
                        pick(e + 4, q)
                        pool.wait_ge(m["cp"], cp_n + (2 * B + 1))
                        passed()
                        gather(e + 4, q)
                        cp_n = cp_n + 1
                    if y_n is not None:
                        pool.wait_ge(m["y"][u], y_n + 8 * B)
                        passed()
                    g.tensor_copy(sidx[:, u, :], slot_i[:, ds(e, 1)]).then_inc(m["cp"], 1)
                    pool.wait_ge(m["cp"], cp_n + (2 * B + 1))
                    pool.wait_ge(m["ya"], e + (B + 1))
                    pool.wait_ge(m["yb"], e + (B + 1))
                    passed()
                    scatter(e, u)

                for e in range(4):
                    step(e, e, 4 + 2 * e, 16 * (e // 2) if e >= 2 else None)
                with pool.Fori(1, NE // 4 - 1) as j:
                    for q in range(4):
                        step(j * 4 + q, q, j * 8 + (4 + 2 * q), (j * 2 + q // 2) * 16)
                xm = MX[i]

                def item_gather(j):
                    c = pool.value_load(item_i[0:1, ds(j + MORE, 1)], min_val=NE, max_val=NT * NE - 1)
                    g.tensor_copy(gidx_i[:, 0, :], slot_g[:, ds(c, 1)])
                    g.tensor_copy(sidx[:, 2, :], slot_i[:, ds(c, 1)]).then_inc(xm["stage"], 1)
                    pool.wait_ge(xm["stage"], stage_n("idx", j))
                    passed()
                    g.indirect_dma_start(out=xg[0], out_offset=None, in_=rows_of,
                                         in_offset=bass.IndirectOffsetOnAxis(ap=gidx_i[:, 0, :], axis=0),
                                         bounds_check=T - 1, oob_is_err=False).then_inc(xm["moved"], 16)

                def item_scatter(j):
                    pool.wait_ge(xm["stage"], stage_n("y", j))
                    passed()
                    g.indirect_dma_start(out=y_rows[i], out_offset=bass.IndirectOffsetOnAxis(ap=sidx[:, 2, :], axis=0),
                                         in_=yo[0], in_offset=None, bounds_check=2 * T - 1,
                                         oob_is_err=False).then_inc(xm["moved"], 16)
                    pool.wait_ge(xm["moved"], j * 32 + 32)

                pool.wait_ge(idx_ok, 2 * i + 2)
                n_x = pool.value_load(nextra[0:1, 0:1], min_val=0, max_val=MORE)
                pool.wait_ge(m["xt_ps"], B + NE - 3)
                with pool.If(n_x > 0):
                    item_gather(0)
                with pool.Else():
                    pool.nop()
                for q in range(4):
                    step(NE - 4 + q, q, 2 * NE - 4 + q, 16 * (NE // 2 - 2 + q // 2), more=False)
                with pool.If(n_x > 0):
                    item_scatter(0)
                with pool.Else():
                    pool.nop()
                with pool.If(n_x > 1):
                    with pool.Fori(1, n_x) as j:
                        item_gather(j)
                        item_scatter(j)
                with pool.Else():
                    pool.nop()
                for u in range(2):
                    pool.wait_ge(m["y"][u], 8 * B + 16 * (NE // 2))
                pool.sem_inc(m["done"], 1)

            experts(0)

            weights_lo(0, H * KD)
            pool.wait_ge(decay_dve, 7)

            def attend(p, split=True):
                pool.wait_ge(fev, p * 4 + 4)
                after(pool, pv_ps, p * 8)
                passed()
                g.tensor_copy(vS, vraw).then_inc(vs_ok, 1)
                after(pool, cb_ps, p * 2)
                g.tensor_copy(nch.rearrange("p a n -> p (a n)"), cumn[:, ds(p * 2 * NT, 2 * NT)]).then_inc(nch_ok, 1)
                for a in range(2):
                    pool.wait_ge(cb_ok, p * 2 + (a + 1))
                    if a == 0:
                        after(pool, sc_ok, p * 8)
                    passed()
                    for qt in range(NT):
                        w = (qt + 1) * P
                        last = g.affine_select(out=cbT[a][:, offs[qt]:offs[qt] + w], in_=cbS[:, a, 0:w], pattern=[[-1, w]],
                                               compare_op=ALU.is_ge, fill=NEG, base=qt * P, channel_multiplier=1)
                    last.then_inc(cbt_ok, 1)
                if split:
                    weights_lo(p % 2, p * KD + (H + 2) * KD)

            weights_lo(1, (H + 1) * KD)
            attend(0)
            with pool.Fori(1, H - 2) as p:
                attend(p)
            for p in range(H - 2, H):
                attend(p, split=False)
            experts(1)


_INS = ['x', 'c', 'ada_w', 'ada_b', 'gdn_w_in', 'gdn_conv', 'gdn_a_log', 'gdn_dt_bias', 'gdn_norm', 'gdn_w_out',
        'fox_w_in', 'fox_b_f', 'fox_q_norm', 'fox_k_norm', 'fox_w_out', 'moe_w_group', 'moe_b_group',
        'moe_w_router', 'moe_b_router', 'moe_w_gate_up', 'moe_w_down', 'final_norm']


def kernel(**inputs):
    import numpy as _np
    import concourse.bacc as _bacc
    from concourse import mybir as _mybir
    from concourse.bass_utils import run_bass_kernel_spmd as _run

    nc = _bacc.Bacc("TRN2", target_bir_lowering=False, num_devices=1)
    arrays, args = {}, []
    for name in _INS:
        a = _np.ascontiguousarray(inputs[name])
        arrays[f"in_{name}_dram"] = a
        args.append(nc.dram_tensor(f"in_{name}_dram", a.shape, _mybir.dt.from_np(a.dtype), kind="ExternalInput").ap())
    args.append(nc.dram_tensor("out_0_dram", (1, T, D), F32, kind="ExternalOutput").ap())
    build(nc, *args)
    r = _run(nc, [arrays], core_ids=[0])
    return r.results[0]["out_0_dram"]
```
